# Optimizing a Trainium2 kernel written in Bass

```python
import math
import jax, jax.numpy as jnp
from jax import lax
import numpy as np

D_MODEL = 1024
BATCH = 1
SEQ = 256
DEPTH = 1

MIX_WIDTH = D_MODEL
FNET_WIDTH = MIX_WIDTH // 2
FNET_GROUPS = 4
FNET_GROUP_DIM = FNET_WIDTH // FNET_GROUPS
HEAD_DIM = 64
N_Q_HEADS = (MIX_WIDTH - FNET_WIDTH) // HEAD_DIM
N_KV_HEADS = 2
GQA_GROUP = N_Q_HEADS // N_KV_HEADS
ATTN_WIDTH = N_Q_HEADS * HEAD_DIM
KV_WIDTH = N_KV_HEADS * HEAD_DIM
IN_WIDTH = FNET_WIDTH + ATTN_WIDTH + 2 * KV_WIDTH
D_FF = 2752
GRID_W = 64
AXIS_DIM = HEAD_DIM // 2
ROPE_THETA = 10000.0
Q_BLOCK = 128
EPS = 1e-6


def rms_norm(x, g):
    xf = x.astype(jnp.float32)
    y = xf * lax.rsqrt(jnp.mean(xf * xf, axis=-1, keepdims=True) + EPS)
    return (y * g.astype(jnp.float32)).astype(x.dtype)

def swiglu(h, w_gate, w_up, w_down):
    return (jax.nn.silu(h @ w_gate) * (h @ w_up)) @ w_down

def axial_rope_tables(seq):
    rows = seq // GRID_W
    row_idx = jnp.repeat(jnp.arange(rows, dtype=jnp.float32), GRID_W)
    col_idx = jnp.tile(jnp.arange(GRID_W, dtype=jnp.float32), rows)
    inv_freq = ROPE_THETA ** (-jnp.arange(0, AXIS_DIM, 2, dtype=jnp.float32) / AXIS_DIM)
    ang_r = row_idx[:, None] * inv_freq[None, :]
    ang_c = col_idx[:, None] * inv_freq[None, :]
    return jnp.cos(ang_r), jnp.sin(ang_r), jnp.cos(ang_c), jnp.sin(ang_c)

def rotate(x, cos, sin):
    half = x.shape[-1] // 2
    x1, x2 = x[..., :half], x[..., half:]
    c = cos[None, :, None, :].astype(x.dtype)
    s = sin[None, :, None, :].astype(x.dtype)
    return jnp.concatenate([x1 * c - x2 * s, x1 * s + x2 * c], axis=-1)

def apply_axial_rope(x, tables):
    cr, sr, cc, sc = tables
    return jnp.concatenate([rotate(x[..., :AXIS_DIM], cr, sr),
                            rotate(x[..., AXIS_DIM:], cc, sc)], axis=-1)

def fourier_mixer(hf, fnet_w, fnet_b):
    b, s, _ = hf.shape
    g = hf.reshape(b, s, FNET_GROUPS, FNET_GROUP_DIM).astype(jnp.float32)
    mixed = jnp.real(jnp.fft.fft2(g, axes=(1, 3), norm="ortho")).astype(hf.dtype)
    out = jnp.einsum('bsgc,gcd->bsgd', mixed, fnet_w) + fnet_b[None, None]
    return out.reshape(b, s, FNET_WIDTH)

def gqa_attention(q, k, v, q_norm, k_norm):
    b, s, _ = q.shape
    q = rms_norm(q.reshape(b, s, N_Q_HEADS, HEAD_DIM), q_norm)
    k = rms_norm(k.reshape(b, s, N_KV_HEADS, HEAD_DIM), k_norm)
    v = v.reshape(b, s, N_KV_HEADS, HEAD_DIM)
    tables = axial_rope_tables(s)
    q = apply_axial_rope(q, tables)
    k = apply_axial_rope(k, tables)
    scale = 1.0 / math.sqrt(HEAD_DIM)
    n_blocks = s // Q_BLOCK
    qb = q.reshape(b, n_blocks, Q_BLOCK, N_KV_HEADS, GQA_GROUP, HEAD_DIM)
    qb = jnp.moveaxis(qb, 1, 0)

    def attend_block(q_blk):
        scores = jnp.einsum('bqhgd,bkhd->bhgqk', q_blk, k).astype(jnp.float32) * scale
        p = jax.nn.softmax(scores, axis=-1).astype(v.dtype)
        return jnp.einsum('bhgqk,bkhd->bqhgd', p, v)

    o = lax.map(attend_block, qb)
    o = jnp.moveaxis(o, 0, 1)
    return o.reshape(b, s, ATTN_WIDTH)

def first_inputs(seed: int = 0) -> dict:
    key = jax.random.key(seed)
    ks = jax.random.split(key, 20)
    D, F = D_MODEL, D_FF
    nrm = lambda k, shape, fan_in: jax.random.normal(k, shape, jnp.float32) * fan_in ** -0.5
    gain = lambda k, n: 1.0 + 0.05 * jax.random.normal(k, (n,), jnp.float32)
    return {
        "x": jax.random.normal(ks[0], (BATCH, SEQ, D), jnp.float32),
        "ffn1_norm": gain(ks[1], D),
        "ffn1_w_gate": nrm(ks[2], (D, F), D),
        "ffn1_w_up": nrm(ks[3], (D, F), D),
        "ffn1_w_down": nrm(ks[4], (F, D), F),
        "mix_norm": gain(ks[5], D),
        "w_in": nrm(ks[6], (D, IN_WIDTH), D),
        "fnet_w": nrm(ks[7], (FNET_GROUPS, FNET_GROUP_DIM, FNET_GROUP_DIM), FNET_GROUP_DIM),
        "fnet_b": 0.02 * jax.random.normal(ks[8], (FNET_GROUPS, FNET_GROUP_DIM), jnp.float32),
        "q_norm": gain(ks[9], HEAD_DIM),
        "k_norm": gain(ks[10], HEAD_DIM),
        "w_out": nrm(ks[11], (MIX_WIDTH, D), MIX_WIDTH),
        "ffn2_norm": gain(ks[12], D),
        "ffn2_w_gate": nrm(ks[13], (D, F), D),
        "ffn2_w_up": nrm(ks[14], (D, F), D),
        "ffn2_w_down": nrm(ks[15], (F, D), F),
        "final_norm": gain(ks[16], D),
    }

def first_block(x, ffn1_norm, ffn1_w_gate, ffn1_w_up, ffn1_w_down, mix_norm, w_in,
              fnet_w, fnet_b, q_norm, k_norm, w_out, ffn2_norm, ffn2_w_gate,
              ffn2_w_up, ffn2_w_down, final_norm):
    for _ in range(DEPTH):
        x = x + 0.5 * swiglu(rms_norm(x, ffn1_norm), ffn1_w_gate, ffn1_w_up, ffn1_w_down)
        h = rms_norm(x, mix_norm)
        u = h @ w_in
        o0 = FNET_WIDTH
        o1 = o0 + ATTN_WIDTH
        o2 = o1 + KV_WIDTH
        f_out = fourier_mixer(u[..., :o0], fnet_w, fnet_b)
        a_out = gqa_attention(u[..., o0:o1], u[..., o1:o2], u[..., o2:], q_norm, k_norm)
        x = x + jnp.concatenate([f_out, a_out], axis=-1) @ w_out
        x = x + 0.5 * swiglu(rms_norm(x, ffn2_norm), ffn2_w_gate, ffn2_w_up, ffn2_w_down)
    return rms_norm(x, final_norm)


DEPTH_2 = 2

N_A = DEPTH_2 // 2
N_B = DEPTH_2 - N_A
CONV_W = 3
N_HEADS = 8
HEAD_DIM_2 = D_MODEL // N_HEADS
BLOCK = 256
TOPK = 3
Q_CHUNK = 32
ROT_DIM = HEAD_DIM_2 // 4
ROPE_THETA_2 = 500000.0
MEM_LEN = 256
MEM_HEADS = 4
MEM_HEAD_DIM = D_MODEL // MEM_HEADS
D_FF_2 = ((8 * D_MODEL + 3 * 256 - 1) // (3 * 256)) * 256


def rms_norm_2(x, g):
    x32 = x.astype(jnp.float32)
    y = x32 * lax.rsqrt(jnp.mean(x32 * x32, axis=-1, keepdims=True) + EPS)
    return (y * g.astype(jnp.float32)).astype(x.dtype)

def rope_cos_sin(positions):
    inv_freq = ROPE_THETA_2 ** (-jnp.arange(0, ROT_DIM, 2, dtype=jnp.float32) / ROT_DIM)
    ang = positions.astype(jnp.float32)[..., None] * inv_freq
    return jnp.cos(ang)[:, :, None, :], jnp.sin(ang)[:, :, None, :]

def apply_partial_rope(x, cos, sin):
    xr = x[..., :ROT_DIM].astype(jnp.float32)
    x1, x2 = xr[..., : ROT_DIM // 2], xr[..., ROT_DIM // 2:]
    rot = jnp.concatenate([x1 * cos - x2 * sin, x2 * cos + x1 * sin], axis=-1)
    return jnp.concatenate([rot.astype(x.dtype), x[..., ROT_DIM:]], axis=-1)

def short_conv_mixer(h, w_in, w_conv, w_out):
    b_gate, c_gate, u = jnp.split(h @ w_in, 3, axis=-1)
    z = c_gate * u
    conv = lax.conv_general_dilated(
        z, w_conv[:, None, :].astype(z.dtype), window_strides=(1,),
        padding=[(CONV_W - 1, 0)], dimension_numbers=("NWC", "WIO", "NWC"),
        feature_group_count=D_MODEL)
    return (b_gate * conv) @ w_out

def mem_cross_attention(h, mem_n, w_q, w_kv, w_o):
    bsz, seq, _ = h.shape
    q = (h @ w_q).reshape(bsz, seq, MEM_HEADS, MEM_HEAD_DIM)
    k, v = jnp.split(mem_n @ w_kv, 2, axis=-1)
    k = k.reshape(bsz, -1, MEM_HEADS, MEM_HEAD_DIM)
    v = v.reshape(bsz, -1, MEM_HEADS, MEM_HEAD_DIM)
    s = jnp.einsum("bshd,bmhd->bhsm", q, k).astype(jnp.float32) * (MEM_HEAD_DIM ** -0.5)
    p = jax.nn.softmax(s, axis=-1).astype(v.dtype)
    o = jnp.einsum("bhsm,bmhd->bshd", p, v).reshape(bsz, seq, D_MODEL)
    return o @ w_o

def swiglu_2(h, w_gu, w_down):
    g, u = jnp.split(h @ w_gu, 2, axis=-1)
    return (jax.nn.silu(g) * u) @ w_down

def shared_kv(x, kv_norm, w_kv, cos, sin):
    bsz, seq, _ = x.shape
    n_blocks = -(-seq // BLOCK)
    pad = n_blocks * BLOCK - seq
    k, v = jnp.split(rms_norm_2(x, kv_norm) @ w_kv, 2, axis=-1)
    k = apply_partial_rope(k.reshape(bsz, seq, N_HEADS, HEAD_DIM_2), cos, sin)
    v = v.reshape(bsz, seq, N_HEADS, HEAD_DIM_2)
    k = jnp.pad(k, ((0, 0), (0, pad), (0, 0), (0, 0)))
    v = jnp.pad(v, ((0, 0), (0, pad), (0, 0), (0, 0)))
    k_blk = k.transpose(0, 2, 1, 3).reshape(bsz, N_HEADS, n_blocks, BLOCK, HEAD_DIM_2)
    v_blk = v.transpose(0, 2, 1, 3).reshape(bsz, N_HEADS, n_blocks, BLOCK, HEAD_DIM_2)
    k_mean = jnp.mean(k_blk.astype(jnp.float32), axis=3)
    return k_blk, v_blk, k_mean

def moba_attention(h, w_q, w_o, cos, sin, k_blk, v_blk, k_mean):
    bsz, seq, _ = h.shape
    n_blocks = k_blk.shape[2]
    k_sel = min(TOPK, n_blocks)
    n_chunks = seq // Q_CHUNK
    scale = HEAD_DIM_2 ** -0.5
    q = apply_partial_rope((h @ w_q).reshape(bsz, seq, N_HEADS, HEAD_DIM_2), cos, sin)
    q_chunks = q.transpose(0, 2, 1, 3).reshape(bsz, N_HEADS, n_chunks, Q_CHUNK, HEAD_DIM_2)
    q_chunks = q_chunks.transpose(2, 0, 1, 3, 4)
    bi = jnp.arange(bsz)[:, None, None, None]
    hi = jnp.arange(N_HEADS)[None, :, None, None]

    def chunk_fn(args):
        c, q_c = args
        qpos = c * Q_CHUNK + jnp.arange(Q_CHUNK)
        qb = (c * Q_CHUNK) // BLOCK
        gate = jnp.einsum("bhqd,bhnd->bhqn", q_c.astype(jnp.float32), k_mean)
        past = jnp.arange(n_blocks) < qb
        gate = jnp.where(past[None, None, None, :], gate, -jnp.inf)
        _, idx = lax.top_k(gate, k_sel)
        valid = idx < qb
        kg = k_blk[bi, hi, idx]
        vg = v_blk[bi, hi, idx]
        s_sel = jnp.einsum("bhqd,bhqrkd->bhqrk", q_c, kg).astype(jnp.float32) * scale
        s_sel = jnp.where(valid[..., None], s_sel, -jnp.inf)
        s_sel = s_sel.reshape(bsz, N_HEADS, Q_CHUNK, k_sel * BLOCK)
        k_own = lax.dynamic_index_in_dim(k_blk, qb, axis=2, keepdims=False)
        v_own = lax.dynamic_index_in_dim(v_blk, qb, axis=2, keepdims=False)
        s_own = jnp.einsum("bhqd,bhkd->bhqk", q_c, k_own).astype(jnp.float32) * scale
        kpos = qb * BLOCK + jnp.arange(BLOCK)
        s_own = jnp.where((kpos[None, :] <= qpos[:, None])[None, None], s_own, -jnp.inf)
        p = jax.nn.softmax(jnp.concatenate([s_sel, s_own], axis=-1), axis=-1)
        p_sel = p[..., : k_sel * BLOCK].reshape(bsz, N_HEADS, Q_CHUNK, k_sel, BLOCK)
        p_own = p[..., k_sel * BLOCK:]
        o = jnp.einsum("bhqrk,bhqrkd->bhqd", p_sel.astype(vg.dtype), vg)
        o = o + jnp.einsum("bhqk,bhkd->bhqd", p_own.astype(v_own.dtype), v_own)
        return o

    out = lax.map(chunk_fn, (jnp.arange(n_chunks, dtype=jnp.int32), q_chunks))
    out = out.transpose(1, 0, 3, 2, 4).reshape(bsz, seq, D_MODEL)
    return out @ w_o

def second_inputs(seed: int = 0) -> dict:
    key = jax.random.key(seed)
    ks = jax.random.split(key, 24)
    f32 = jnp.float32

    def w(k, shape, fan_in):
        return jax.random.normal(k, shape, f32) * (fan_in ** -0.5)

    def gain(k, shape):
        return 1.0 + 0.02 * jax.random.normal(k, shape, f32)

    x = jax.random.normal(ks[0], (BATCH, SEQ, D_MODEL), f32)
    mem = jax.random.normal(ks[1], (BATCH, MEM_LEN, D_MODEL), f32)
    offset = jax.random.randint(ks[2], (BATCH, 1), 0, 8192, dtype=jnp.int32)
    positions = offset + jnp.arange(SEQ, dtype=jnp.int32)[None, :]
    return {
        "x": x,
        "mem": mem,
        "positions": positions,
        "norm_mix": gain(ks[3], (DEPTH_2, D_MODEL)),
        "norm_mem": gain(ks[4], (DEPTH_2, D_MODEL)),
        "norm_memkv": gain(ks[5], (DEPTH_2, D_MODEL)),
        "norm_ffn": gain(ks[6], (DEPTH_2, D_MODEL)),
        "norm_final": gain(ks[7], (D_MODEL,)),
        "conv_w_in": w(ks[8], (N_A, D_MODEL, 3 * D_MODEL), D_MODEL),
        "conv_w": w(ks[9], (N_A, CONV_W, D_MODEL), CONV_W),
        "conv_w_out": w(ks[10], (N_A, D_MODEL, D_MODEL), D_MODEL),
        "kv_norm": gain(ks[11], (D_MODEL,)),
        "w_kv": w(ks[12], (D_MODEL, 2 * D_MODEL), D_MODEL),
        "moba_w_q": w(ks[13], (N_B, D_MODEL, D_MODEL), D_MODEL),
        "moba_w_o": w(ks[14], (N_B, D_MODEL, D_MODEL), D_MODEL),
        "mem_w_q": w(ks[15], (DEPTH_2, D_MODEL, D_MODEL), D_MODEL),
        "mem_w_kv": w(ks[16], (DEPTH_2, D_MODEL, 2 * D_MODEL), D_MODEL),
        "mem_w_o": w(ks[17], (DEPTH_2, D_MODEL, D_MODEL), D_MODEL),
        "ffn_w_gu": w(ks[18], (DEPTH_2, D_MODEL, 2 * D_FF_2), D_MODEL),
        "ffn_w_down": w(ks[19], (DEPTH_2, D_FF_2, D_MODEL), D_FF_2),
    }

def second_block(x, mem, positions, norm_mix, norm_mem, norm_memkv, norm_ffn, norm_final,
              conv_w_in, conv_w, conv_w_out, kv_norm, w_kv, moba_w_q, moba_w_o,
              mem_w_q, mem_w_kv, mem_w_o, ffn_w_gu, ffn_w_down):
    cos, sin = rope_cos_sin(positions)
    k_blk = v_blk = k_mean = None
    for l in range(DEPTH_2):
        h = rms_norm_2(x, norm_mix[l])
        if l < N_A:
            x = x + short_conv_mixer(h, conv_w_in[l], conv_w[l], conv_w_out[l])
        else:
            j = l - N_A
            x = x + moba_attention(h, moba_w_q[j], moba_w_o[j], cos, sin, k_blk, v_blk, k_mean)
        x = x + mem_cross_attention(rms_norm_2(x, norm_mem[l]), rms_norm_2(mem, norm_memkv[l]),
                                    mem_w_q[l], mem_w_kv[l], mem_w_o[l])
        x = x + swiglu_2(rms_norm_2(x, norm_ffn[l]), ffn_w_gu[l], ffn_w_down[l])
        if l == N_A - 1:
            k_blk, v_blk, k_mean = shared_kv(x, kv_norm, w_kv, cos, sin)
    return rms_norm_2(x, norm_final)


def setup_inputs(seed=0):
    out = dict(first_inputs(seed))
    for name, value in second_inputs(seed + 1).items():
        if name != "x":
            out[name + "_2"] = value
    return out


def reference(
    x, ffn1_norm, ffn1_w_gate, ffn1_w_up, ffn1_w_down, mix_norm, w_in, fnet_w, fnet_b, q_norm,
    k_norm, w_out, ffn2_norm, ffn2_w_gate, ffn2_w_up, ffn2_w_down, final_norm, mem_2,
    positions_2, norm_mix_2, norm_mem_2, norm_memkv_2, norm_ffn_2, norm_final_2, conv_w_in_2,
    conv_w_2, conv_w_out_2, kv_norm_2, w_kv_2, moba_w_q_2, moba_w_o_2, mem_w_q_2, mem_w_kv_2,
    mem_w_o_2, ffn_w_gu_2, ffn_w_down_2,
):
    x = first_block(
        x, ffn1_norm, ffn1_w_gate, ffn1_w_up, ffn1_w_down, mix_norm, w_in, fnet_w, fnet_b,
        q_norm, k_norm, w_out, ffn2_norm, ffn2_w_gate, ffn2_w_up, ffn2_w_down, final_norm,
    )
    return second_block(
        x, mem_2, positions_2, norm_mix_2, norm_mem_2, norm_memkv_2, norm_ffn_2, norm_final_2,
        conv_w_in_2, conv_w_2, conv_w_out_2, kv_norm_2, w_kv_2, moba_w_q_2, moba_w_o_2,
        mem_w_q_2, mem_w_kv_2, mem_w_o_2, ffn_w_gu_2, ffn_w_down_2,
    )


_drawn_inputs = setup_inputs


def setup_inputs(seed=0):
    import zlib

    import numpy as np

    out = dict(_drawn_inputs(seed))
    spreads = {}
    factors = {'fnet_b': 2.73,
     'q_norm': 8.0,
     'k_norm': 8.0,
     'norm_mem_2': 8.0,
     'norm_memkv_2': 8.0,
     'norm_ffn_2': 3.566,
     'norm_final_2': 2.799,
     'kv_norm_2': 8.0}
    for name, (base, spread) in spreads.items():
        noise = np.random.default_rng([zlib.crc32(name.encode()), seed]).standard_normal(out[name].shape)
        drawn = base * np.exp(spread * noise) if base else spread * noise
        out[name] = __import__('jax').numpy.asarray(drawn.astype(out[name].dtype))
    for name, factor in factors.items():
        out[name] = (out[name] * factor).astype(out[name].dtype)
    return out
```

```python
from contextlib import ExitStack

import numpy as np
import concourse.bass as bass
from concourse import mybir

F32 = mybir.dt.float32
F32R = mybir.dt.float32r
I32 = mybir.dt.int32
ALU = mybir.AluOpType
ACT = mybir.ActivationFunctionType
AX = mybir.AxisListType

P = 128
S = 256
D = 1024
KB = D // P
KP = KB // 2
NT = S // P
TILE = 16
RING = 3
FF = 22
PEEL = 4
EPS = 1e-6
GQ_DIM, MEM_DIM, MOBA_DIM = 64, 256, 128
GQ_HEADS = 10

MEM0 = [("v", 0), ("q", 0), ("q", 1), ("q", 2), ("q", 3), ("v", 1), ("v", 2), ("v", 3)]
MOBA = [("k", 0), ("k", 1), ("q", 0), ("q", 1), ("v", 0), ("k", 2), ("q", 2), ("v", 1), ("k", 3), ("q", 3), ("v", 2), ("v", 3)]
MEM1 = [("k", 0), ("k", 1), ("q", 0), ("q", 1), ("v", 0), ("k", 2), ("q", 2), ("k", 3), ("q", 3), ("v", 1), ("v", 2), ("v", 3)]
GQA = [("k", j) for j in range(KP)]
PARTS = {"gqa": GQA, "mem0": MEM0, "moba": MOBA, "mem1": MEM1}
STREAM = [
    ("gu0", FF), ("down0", FF // 2), ("w_in", 5), ("gqa", len(GQA)), ("w_out", KP),
    ("gu1", FF), ("down1", FF // 2), ("conv_in", 12), ("conv_out", KP),
    ("mem0", len(MEM0)), ("mem_o0", KP), ("gu2", FF), ("down2", FF // 2),
    ("moba", len(MOBA)), ("moba_o", KP), ("mem1", len(MEM1)), ("mem_o1", KP), ("gu3", FF), ("down3", FF // 2),
]
WRITES = ["down0", "w_out", "down1", "conv_out", "mem_o0", "down2", "moba_o", "mem_o1", "down3"]
WRITE = {n: i for i, n in enumerate(WRITES)}
DOWNS = {n: i for i, n in enumerate([w for w in WRITES if w.startswith("down")])}
FIRST, COUNT, ROT = {}, {}, {}
_t = _r = 0
for _name, _n in STREAM:
    FIRST[_name], COUNT[_name], ROT[_name] = _t, _n, _r
    _t += _n
    _r += 0 if _name in WRITE else _n
TILES = _t

AHEAD = {"gqa": 1, "mem0": 4, "moba": 5, "mem1": 5}
PIECES = {
    "gqa": {0: ([(1, 0, 3)], [(1, 3, 6)]), 1: ([], [(1, 6, 8), (2, 0, 1)]), 2: ([], [(2, 1, 4)]), 3: ([], [(2, 4, 7)]),
            4: ([], [(2, 7, 8), (3, 0, 2)]), 5: ([], [(3, 2, 4)]), 6: ([], [(3, 4, 6)]), 7: ([], [(3, 6, 8)])},
    "mem0": {0: ([(4, 0, 4)], [(4, 4, 8), (5, 0, 4)]), 1: ([], [(5, 4, 8), (6, 0, 4)]), 2: ([], [(6, 4, 8), (7, 0, 5)]),
             3: ([(7, 5, 8)], [])},
    "moba": {0: ([(5, 0, 4)], [(5, 4, 8), (6, 0, 6)]),
             1: ([], [("k", 2), (6, 6, 8), (7, 0, 4), ("q", 2), (7, 4, 6)]),
             2: ([], [(7, 6, 8), (8, 0, 8)]),
             3: ([], [(9, 0, 2), ("k", 3), (9, 2, 8), (10, 0, 2), ("q", 3), (10, 2, 4)]),
             4: ([], [(10, 4, 8), (11, 0, 2)]), 5: ([], [(11, 2, 5)]), 6: ([(11, 5, 8)], [])},
    "mem1": {0: ([(5, 0, 8), (6, 0, 8), (7, 0, 2)], [(7, 2, 8), (8, 0, 8)]), 1: ([], [(9, 0, 8), (10, 0, 3)]),
             2: ([], [(10, 3, 8), (11, 0, 4)]), 3: ([(11, 4, 8)], [])},
}
ROPES = [("k", 0), ("k", 1), ("q", 0), ("q", 1), ("k", 2), ("q", 2), ("k", 3), ("q", 3)]

VECTORS = [("ffn1_norm", KB), ("mix_norm", KB), ("ffn2_norm", KB), ("final_norm", KB), ("norm_mix0", KB),
           ("norm_mix1", KB), ("norm_mem0", KB), ("norm_mem1", KB), ("norm_memkv0", KB), ("norm_memkv1", KB),
           ("norm_ffn0", KB), ("norm_ffn1", KB), ("norm_final", KB), ("kv_norm", KB), ("conv_w", 3 * KB),
           ("fnet_b", 4), ("q_norm", 1), ("k_norm", 1)]
CONSTS = [("rotate", P), ("head_ones", 2), ("ident", P), ("axial_cos", S), ("axial_sin", S), ("causal", P), ("inv_freq", 1)]
FOURIER = [("dft_feature", 2 * P), ("dft_cos", NT * S), ("dft_sin", NT * S)]


def columns(table):
    at, out = 0, {}
    for name, n in table:
        out[name] = (at, at + n)
        at += n
    return out, at


VCOL, NV = columns(VECTORS)
CCOL, NC = columns(CONSTS)
FCOL, NF = columns(FOURIER)

SUMS = ["x0", "mem", "mix", "ffn2", "mix0", "mem0", "ffn0", "mix1", "mem1", "ffn1", "final"]
SUM = {n: i for i, n in enumerate(SUMS)}
FOLDED = [n for n in SUMS if n not in ("mix0", "final")]
FOLD = {n: i for i, n in enumerate(FOLDED)}
OPERANDS = ["x0", "memkv0", "mix", "ffn2", "mix0", "mem0", "ffn0", "memkv1", "kv", "mix1", "mem1", "ffn1"]
OPERAND = {n: i for i, n in enumerate(OPERANDS)}

GQ_UNITS = [(b, half) for b in range(4) for half in range(2)]
UNITS = {"gqa": 8, "mem0": 4, "moba": 8, "mem1": 4}
UNIT0 = {"gqa": 0, "mem0": 8, "moba": 12, "mem1": 20}
SCALE = {"gqa": GQ_DIM ** -0.5, "mem0": MEM_DIM ** -0.5, "moba": MOBA_DIM ** -0.5, "mem1": MEM_DIM ** -0.5}

TWO_PI = 2 * np.pi
_C1 = 6.28125
_C2 = float(np.round((TWO_PI - _C1) * 2 ** 17) / 2 ** 17)
_C3 = float(np.round((TWO_PI - _C1 - _C2) * 2 ** 26) / 2 ** 26)
TURN = (_C1, _C2, _C3, float(TWO_PI - _C1 - _C2 - _C3))
ROUND = 1.5 * 2 ** 23
PI_BELOW = 3.1415925
ROOT_GUESS = float(0x5F3759DF)
ROOT_STEPS = 3


def program(nc, weights, x_t, mem_t, vectors, consts, fourier, fnet_w, positions, out_t):
    ctx = ExitStack()
    with ctx:
        def sb(name, shape, dt=F32):
            return ctx.enter_context(nc.sbuf_tensor(name, shape, dt))

        def sem(name):
            return ctx.enter_context(nc.semaphore(name))

        raw = [sb(f"raw{i}", [P, TILE, P]) for i in range(RING)]
        w_hi = [sb(f"w_hi{i}", [P, TILE, P], F32R) for i in range(RING)]
        w_lo = [sb(f"w_lo{i}", [P, TILE, P], F32R) for i in range(RING)]
        x = sb("x", [P, KB, S])
        mem = sb("mem", [P, KB, S])
        work = sb("work", [P, KB, S])
        xn_hi = sb("xn_hi", [P, KB, S], F32R)
        xn_lo = sb("xn_lo", [P, KB, S], F32R)
        mn_hi = sb("mn_hi", [P, KB, S], F32R)
        mn_lo = sb("mn_lo", [P, KB, S], F32R)
        h_hi = sb("h_hi", [P, FF, S], F32R)
        h_lo = sb("h_lo", [P, FF, S], F32R)
        q_t = sb("q_t", [P, KB, S])
        k_t = sb("k_t", [P, KB, S])
        v_s = sb("v_s", [P, NT, D])
        vec = sb("vec", [P, NV])
        con = sb("con", [P, NC])
        ones = sb("ones", [P, P])
        gain2 = sb("gain2", [P, KB])
        weigh = sb("weigh", [P, KB, 2])
        m_cos = sb("m_cos", [32, S])
        m_sin = sb("m_sin", [32, S])
        pos = m_cos[:].bitcast(I32)
        r_x = sb("r_x", [P, S])
        r_m = sb("r_m", [P, S])
        diag = sb("diag", [P, NT, P])
        scratch = sb("scratch", [P, 8, S])
        small = sb("small", [P, 2, 4, NT])
        root = sb("root", [P, 3, 2 * GQ_HEADS])
        col_x = sb("col_x", [P, NT])
        col_m = sb("col_m", [P, NT])
        col_1 = sb("col_1", [P, NT])
        z_s = sb("z_s", [P, 2, S + 2])

        gu_s = [scratch[:, 2 * i:2 * i + 2, :] for i in range(3)]
        probs = [scratch[:, 2 * i:2 * i + 2, :] for i in range(2)]
        probs_t = [scratch[:, 4 + 2 * i:6 + 2 * i, :] for i in range(2)]
        conv_s = [scratch[:, 0:2, :], scratch[:, 2:4, :]]
        tap_s = scratch[:, 4:6, :]
        gv_t, gk_t, f_w = q_t[:, 4, :], q_t[:, 5, :], q_t[:, 6:8, :].rearrange("p a (b d) -> p (a b) d", d=P)
        dft_feature = v_s[:, 0, 2 * P:4 * P]
        dft_cos = v_s[:, 0, 512:1024].rearrange("p (t s) -> p t s", t=NT)
        dft_sin = v_s[:, 1, 512:1024].rearrange("p (t s) -> p t s", t=NT)

        bank = [ctx.enter_context(nc.psum_tensor(f"bank{i}", [P, 2, S], F32)) for i in range(8)]
        rot = bank[0:3]
        stat_bank = bank[3]
        acc = bank[4:8]

        def v(name, i=0):
            if name == "gain2":
                return gain2[:, i:i + 1]
            a = VCOL[name][0] + i
            return vec[:, a:a + 1]

        def c(name):
            a, b = CCOL[name]
            return con[:, a:b]

        def both(t, n=2, rows=P):
            return t.rearrange("p (o s) -> p o s", o=1).to_broadcast([rows, n, S])

        def rows_of(tile, k0, k1):
            return tile.rearrange("p (m k) c -> p m k c", m=2)[:, :, k0:k1, :]

        def pair(b):
            return slice(2 * b, 2 * b + 2)

        landed = [sem(f"weights_landed{i}") for i in range(RING)]
        start_landed = [sem(f"start_landed{i}") for i in range(KP + 2)]
        start_hi, start_lo = sem("start_hi"), sem("start_lo")
        x_landed = [sem(f"x_landed{b}") for b in range(KP)]
        vec_landed, mem_landed, const_landed = sem("vec_landed"), sem("mem_landed"), sem("const_landed")
        fourier_landed = sem("fourier_landed")
        ones_set, pads_set = sem("ones_set"), sem("pads_set")
        weight_hi, weight_lo = sem("weight_hi"), sem("weight_lo")
        tile_done = sem("tile_done")
        drained = sem("drained")
        acc_done = sem("acc_done")
        gated, whole, h_rounded, h_split = sem("gated"), sem("whole"), sem("h_rounded"), sem("h_split")
        written = sem("written")
        rounded, split_done = sem("rounded"), sem("split_done")
        squared, folded, summed = sem("squared"), sem("folded"), sem("summed")
        factor, spread, spread_read = sem("factor"), sem("spread"), sem("spread_read")
        linked = sem("linked")
        trig_ready, trig_done = sem("trig_ready"), sem("trig_done")
        qk_squared, qk_sum, qk_root, qk_spread, qk_normed, qk_rotated, qk_done = (
            sem(n) for n in ("qk_squared", "qk_sum", "qk_root", "qk_spread", "qk_normed", "qk_rotated", "qk_done"))
        v_turned, v_copied = sem("v_turned"), sem("v_copied")
        f_feat, f_feat_copied, f_seq, f_seq_copied, f_out, f_rounded, f_split = (
            sem(n) for n in ("f_feat", "f_feat_copied", "f_seq", "f_seq_copied", "f_out", "f_rounded", "f_split"))
        a_scores, a_max, a_exp, a_probs, a_turned, a_turned_copied, a_out, a_rounded, a_split = (
            sem(n) for n in ("a_scores", "a_max", "a_exp", "a_probs", "a_turned", "a_turned_copied", "a_out",
                             "a_rounded", "a_split"))
        y_whole, y_rounded, y_split = sem("y_whole"), sem("y_rounded"), sem("y_split")
        rope_rotated, rope_done = sem("rope_rotated"), sem("rope_done")
        out_ready, stored = sem("out_ready"), sem("stored")

        CONST_DMAS = 2 * 16
        FOURIER_DMAS = 4 * 16

        def plan(kind):
            units = []
            for n in range(UNITS[kind]):
                if kind == "gqa":
                    b, half = GQ_UNITS[n]
                    rows = slice(half * GQ_DIM, (half + 1) * GQ_DIM)
                    units.append(dict(q=[q_t[rows, b, :]], k=[gk_t[rows, :]], v=[v_s[:, :, 0:P]],
                                      rows=rows, blocks=(4 + b, 5 + b), causal=False))
                elif kind == "moba":
                    units.append(dict(q=[q_t[:, n, :]], k=[k_t[:, n, :]], v=[v_s[:, :, n * P:(n + 1) * P]],
                                      rows=slice(0, P), blocks=(n, n + 1), causal=True, v_tile=MOBA.index(("v", n // 2))))
                else:
                    parts = PARTS[kind]
                    units.append(dict(q=[q_t[:, 2 * n + i, :] for i in range(2)],
                                      k=[k_t[:, 2 * n + i, :] for i in range(2)],
                                      v=[v_s[:, :, (2 * n + i) * P:(2 * n + i + 1) * P] for i in range(2)],
                                      rows=slice(0, P), blocks=(2 * n, 2 * n + 2), causal=False,
                                      qk_tile=max(parts.index(p) for p in (("q", n), ("k", n)) if p in parts),
                                      v_tile=parts.index(("v", n))))
            return units

        def ended(kind, n, i):
            return [piece[0] for piece in PIECES[kind].get(n, ([], []))[i] if piece[-1] == KB]

        block = ctx.enter_context(nc.Block())

        @block.sync
        def _(sp):
            for b in range(KP):
                sp.dma_start(rows_of(raw[0][:], 2 * b, 2 * b + 2), rows_of(weights[0], 2 * b, 2 * b + 2)).then_inc(start_landed[b], 16)
            for i in range(2):
                a, b = i * KB // 2, (i + 1) * KB // 2
                sp.dma_start(rows_of(raw[1][:], a, b), rows_of(weights[1], a, b)).then_inc(start_landed[KP + i], 16)
            sp.dma_start(raw[2][:], weights[2]).then_inc(landed[2], 16)
            sp.dma_start(con[:], consts).then_inc(const_landed, 16)
            sp.dma_start(mem[:], mem_t).then_inc(mem_landed, 16)
            sp.dma_start(pos, positions).then_inc(const_landed, 16)
            with sp.Fori(1, 4) as i:
                for s in range(RING):
                    sp.wait_ge(weight_lo, RING * i + s - RING + 1)
                    sp.dma_start(raw[s][:], weights[RING * i + s]).then_inc(landed[s], 16)
            for name, dst in (("dft_feature", v_s[:, 0, 256:512]), ("dft_cos", v_s[:, 0, 512:1024]),
                              ("dft_sin", v_s[:, 1, 512:1024])):
                a, b = FCOL[name]
                sp.dma_start(dst, fourier[:, a:b]).then_inc(fourier_landed, 16)
            sp.dma_start(f_w, fnet_w).then_inc(fourier_landed, 16)
            with sp.Fori(4, TILES // RING) as i:
                for s in range(RING):
                    sp.wait_ge(weight_lo, RING * i + s - RING + 1)
                    sp.dma_start(raw[s][:], weights[RING * i + s]).then_inc(landed[s], 16)
            for t in range(TILES // RING * RING, TILES):
                sp.wait_ge(weight_lo, t - RING + 1)
                sp.dma_start(raw[t % RING][:], weights[t]).then_inc(landed[t % RING], 16)
            for b in range(KP):
                sp.wait_ge(out_ready, b + 1)
                sp.dma_start(out_t[:, pair(b), :], work[:, pair(b), :]).then_inc(stored, 16)
            sp.wait_ge(stored, 16 * KP)

        @block.gpsimd
        def _(pool):
            pool.memset(ones[:], 1.0).then_inc(ones_set, 1)
            pool.memset(weigh[:, :, 0:1], 1.0).then_inc(ones_set, 1)
            pool.memset(z_s[:, :, 0:2], 0.0).then_inc(pads_set, 1)
            for i, name in enumerate(FOLDED):
                for b in range(1, KP):
                    pool.wait_ge(squared, KP * SUM[name] + b + 1)
                    if b > 1:
                        pool.wait_ge(folded, (KP - 1) * i + b - 1)
                    pool.tensor_tensor(work[:, 0:2, :], work[:, 0:2, :], work[:, pair(b), :], ALU.add).then_inc(folded, 1)

        @block.tensor
        def _(pe):
            def products(out, hi, lo, rhs_hi, rhs_lo, first, last):
                pe.matmul(out, hi, rhs_hi, start=first, stop=False, skip_group_check=True)
                pe.matmul(out, hi, rhs_lo, start=False, stop=False, skip_group_check=True)
                return pe.matmul(out, lo, rhs_hi, start=False, stop=last, skip_group_check=True)

            def square_tile(t, out, a_hi, a_lo, slot=None, ready=None, beside={}, in_parts=False, ks=(0, KB)):
                slot = t % RING if slot is None else slot
                if ks[0] == 0 and not in_parts:
                    pe.wait_ge(weight_lo, t + 1)
                for k in range(*ks):
                    if ready is not None:
                        for s, value in ready(k):
                            pe.wait_ge(s, value)
                    if k in beside:
                        beside[k]()
                    for m in range(2):
                        mm = products(out[:, m, :], w_hi[slot][:, m * KB + k, :], w_lo[slot][:, m * KB + k, :],
                                      a_hi[:, k, :], a_lo[:, k, :], k == 0 and m == 0, k == KB - 1)
                if ks[1] == KB:
                    mm.then_inc(tile_done, 1)

            def value_tile(t, out, a_hi, a_lo, beside={}, ks=(0, KB)):
                wh, wl = (w[t % RING][:].rearrange("p (m k) c -> p k m c", m=2) for w in (w_hi, w_lo))
                if ks[0] == 0:
                    pe.wait_ge(weight_lo, t + 1)
                for k in range(*ks):
                    if k in beside:
                        beside[k]()
                    for n in range(NT):
                        o = out[:, n, :].rearrange("p (m c) -> p m c", m=2)
                        mm = products(o, a_hi[:, k, n * P:(n + 1) * P], a_lo[:, k, n * P:(n + 1) * P],
                                      wh[:, k], wl[:, k], k == 0 and n == 0, k == KB - 1)
                if ks[1] == KB:
                    mm.then_inc(tile_done, 1)

            def operand(name):
                return lambda k: [(split_done, KP * OPERAND[name] + k // 2 + 1)] if k % 2 == 0 else []

            def rotating(name, j, fresh=True):
                r = ROT[name] + j
                if r >= 3 and fresh:
                    pe.wait_ge(drained, r - 2)
                return rot[r % 3]

            def sums(name):
                pe.wait_ge(ones_set, 2)
                if SUM[name]:
                    pe.wait_ge(spread_read, SUM[name])
                blocks, cols = (2, 1) if name in FOLD else (KB, 2) if name == "mix0" else (KB, 1)
                if name in FOLD:
                    pe.wait_ge(folded, (KP - 1) * (FOLD[name] + 1))
                for k in range(blocks):
                    if name not in FOLD and k % 2 == 0:
                        pe.wait_ge(squared, KP * SUM[name] + k // 2 + 1)
                    for n in range(NT):
                        mm = pe.matmul(stat_bank[:, 0, cols * n:cols * (n + 1)], work[:, k, n * P:(n + 1) * P],
                                       weigh[:, k, 0:cols], start=k == 0 and n == 0, stop=k == blocks - 1,
                                       skip_group_check=True)
                mm.then_inc(summed, 1)

            def spread_diagonal(count, half):
                pe.wait_ge(factor, count)
                for t in range(NT):
                    mm = pe.matmul(stat_bank[:, half, t * P:(t + 1) * P], ones[:], diag[:, t, :], start=True, stop=True)
                mm.then_inc(spread, 1)

            def spread_factor(name):
                spread_diagonal(SUM[name] + (2 if SUM[name] > SUM["mix0"] else 1), 1)

            def norm(name):
                return {1: {3: lambda: sums(name)}, 2: {2: lambda: spread_factor(name)}}

            def gate_up(n, name):
                phase = f"gu{n}"
                t0, r0 = FIRST[phase], ROT[phase]
                for j in range(PEEL):
                    ready = operand(name) if j == 0 else None
                    if n == 0 and j < 2:
                        ready = ((lambda k: operand(name)(k) + ([(start_lo, k // 2 + 1)] if k in (0, 2, 4) else [(weight_lo, 1)] if k == 6 else []))
                                 if j == 0 else (lambda k: [(start_lo, KP)] if k == 0 else [(weight_lo, 2)] if k == KB // 2 else []))
                    square_tile(t0 + j, rotating(phase, j), xn_hi, xn_lo, ready=ready, in_parts=n == 0 and j < 2,
                                beside=norm(name).get(j, {}))
                with pe.Fori(0, (FF - PEEL) // 3) as i:
                    for q in range(3):
                        pe.wait_ge(drained, 3 * i + (r0 + PEEL + q - 2))
                        square_tile(3 * i + (t0 + PEEL + q), rot[(r0 + PEEL + q) % 3], xn_hi, xn_lo,
                                    slot=(t0 + PEEL + q) % RING)

            def down(n, early=None, late=None):
                t0 = FIRST[f"down{n}"]
                w = WRITE[f"down{n}"]

                def blocks(slot, row, order, start, stop):
                    for k, m in order:
                        mm = products(acc[m // 2][:, m % 2, :], w_hi[slot][:, k * KB + m, :], w_lo[slot][:, k * KB + m, :],
                                      h_hi[:, row + k, :], h_lo[:, row + k, :], start and k == 0 and m % 2 == 0, stop and k == 1)
                        if stop and k == 1 and m % 2 and m < KB - 1:
                            mm.then_inc(acc_done, 1)
                    mm.then_inc(tile_done, 1)

                by_row = [(k, m) for k in range(2) for m in range(KB)]
                pe.wait_ge(weight_lo, t0 + 1)
                pe.wait_ge(h_split, FF * n + 2)
                if w:
                    pe.wait_ge(written, KP * w)
                blocks(t0 % RING, 0, by_row, True, False)
                if early:
                    early()
                with pe.Fori(0, FF // 2 // 3) as i:
                    for q in range(3):
                        pe.wait_ge(weight_lo, 3 * i + (t0 + 2 + q))
                        pe.wait_ge(h_split, 6 * i + (FF * n + 2 * (2 + q)))
                        blocks((t0 + 1 + q) % RING, 6 * i + 2 * (1 + q), by_row, False, False)
                if late:
                    late()
                pe.wait_ge(weight_lo, t0 + FF // 2)
                pe.wait_ge(h_split, FF * n + FF)
                blocks((t0 + FF // 2 - 1) % RING, FF - 2, [(k, m) for m in range(KB) for k in range(2)], False, True)

            def residual(name, ready):
                pe.wait_ge(written, KP * WRITE[name])
                for b in range(KP):
                    square_tile(FIRST[name] + b, acc[b], h_hi, h_lo, ready=ready if b == 0 else None)

            def part(kind, j, ks=(0, KB), **more):
                what = PARTS[kind][j][0]
                t, out = FIRST[kind] + j, rotating(kind, j, ks[0] == 0)
                if kind == "moba":
                    src = (h_hi[:, KB:2 * KB, :], h_lo[:, KB:2 * KB, :]) if what == "q" else (xn_hi, xn_lo)
                else:
                    src = (xn_hi, xn_lo) if what == "q" else (mn_hi, mn_lo)
                if what == "v":
                    value_tile(t, out, *src, ks=ks, beside=more.get("beside", {}))
                else:
                    square_tile(t, out, *src, ks=ks, **more)

            def rotate_group(what, j):
                g, part_t = ROPES.index((what, j)), k_t if what == "k" else q_t
                pe.wait_ge(drained, ROT["moba"] + MOBA.index((what, j)) + 1)
                if g:
                    pe.wait_ge(rope_done, g)
                else:
                    pe.wait_ge(spread_read, SUM["mix1"] + 1)
                pe.matmul(stat_bank[0:32], c("rotate")[0:32, 0:32], part_t[0:32, pair(j), :],
                          start=True, stop=True).then_inc(rope_rotated, 1)

            def attention(kind):
                u0, units = UNIT0[kind], plan(kind)

                def pieces(n, i):
                    for piece in PIECES[kind].get(n, ([], []))[i]:
                        if piece in ROPES:
                            rotate_group(*piece)
                        else:
                            part(kind, piece[0], ks=piece[1:])

                def scores(n):
                    u, a = u0 + n, units[n]
                    if u >= 2:
                        pe.wait_ge(a_exp, u - 1)
                    if "qk_tile" in a:
                        pe.wait_ge(drained, ROT[kind] + a["qk_tile"] + 1)
                    if kind == "moba":
                        pe.wait_ge(rope_done, ROPES.index(("q", n // 2)) + 1)
                    if kind == "gqa":
                        pe.wait_ge(qk_done, 2 if n < 4 else 3)
                    for t in range(NT):
                        keys = (t + 1) * P if a["causal"] else S
                        for i, (q, k) in enumerate(zip(a["q"], a["k"])):
                            mm = pe.matmul(acc[u % 2][:, t, 0:keys], q[:, t * P:(t + 1) * P], k[:, 0:keys],
                                           start=i == 0, stop=i == len(a["q"]) - 1)
                    mm.then_inc(a_scores, 1)

                scores(0)
                scores(1)
                for n, a in enumerate(units):
                    u = u0 + n
                    pieces(n, 0)
                    pe.wait_ge(a_probs, u + 1)
                    if u:
                        pe.wait_ge(a_turned_copied, u)
                    for t in range(NT):
                        for kt in range(t + 1 if a["causal"] else NT):
                            mm = pe.transpose(acc[2][:, kt, t * P:(t + 1) * P], probs[u % 2][:, t, kt * P:(kt + 1) * P],
                                              c("ident"))
                    mm.then_inc(a_turned, 1)
                    if n + 2 < len(units):
                        scores(n + 2)
                    pieces(n, 1)
                    if "v_tile" in a:
                        pe.wait_ge(drained, ROT[kind] + a["v_tile"] + 1)
                    pe.wait_ge(a_turned_copied, u + 1)
                    if u:
                        pe.wait_ge(a_split, u)
                    for i, val in enumerate(a["v"]):
                        for kt in range(NT):
                            q0 = kt * P if a["causal"] else 0
                            mm = pe.matmul(acc[3][:, i, q0:S], val[:, kt, :], probs_t[u % 2][:, kt, q0:S],
                                           start=kt == 0, stop=kt == NT - 1, skip_group_check=True)
                    mm.then_inc(a_out, 1)

            gate_up(0, "x0")
            down(0, early=lambda: sums("mem"), late=lambda: spread_factor("mem"))
            pe.wait_ge(const_landed, CONST_DMAS)
            qk = [gk_t, q_t[:, 0:2, :], q_t[:, 2:4, :]]
            qk_sq = [work[:, 4, :], work[:, 5, :], work[:, 6, :], scratch[:, 6, :], scratch[:, 7, :]]

            def head_sums():
                pe.wait_ge(qk_squared, 3)
                for t in range(NT):
                    for b in range(GQ_HEADS // 2):
                        at = GQ_HEADS * t + 2 * b
                        mm = pe.matmul(stat_bank[:, 0, at:at + 2], qk_sq[b][:, t * P:(t + 1) * P], c("head_ones"),
                                       start=True, stop=True)
                mm.then_inc(qk_sum, 1)

            for j in range(5):
                square_tile(FIRST["w_in"] + j, rotating("w_in", j), xn_hi, xn_lo, ready=operand("mix") if j == 0 else None,
                            beside={**norm("mix"), 3: {5: head_sums}}.get(j, {}))
            for n in range(NT):
                mm = pe.transpose(acc[3][:, 0, n * P:(n + 1) * P], gv_t[:, n * P:(n + 1) * P], c("ident"))
            mm.then_inc(v_turned, 1)

            def feature_sums(g):
                pe.wait_ge(drained, ROT["w_in"] + 5)
                if g:
                    pe.wait_ge(f_feat_copied, g)
                for n in range(NT):
                    mm = pe.matmul(rot[1][:, n, :], work[:, g, n * P:(n + 1) * P], dft_feature, start=True, stop=True)
                mm.then_inc(f_feat, 1)

            pe.wait_ge(fourier_landed, FOURIER_DMAS)
            feature_sums(0)
            pe.wait_ge(qk_root, 1)
            for h in range(GQ_HEADS):
                b, rows = h // 2, slice(h % 2 * GQ_DIM, (h % 2 + 1) * GQ_DIM)
                for t in range(NT):
                    at = GQ_HEADS * t + h
                    mm = pe.matmul(acc[(b + 1) // 2][rows, (b + 1) % 2, t * P:(t + 1) * P],
                                   root[:, 1, at:at + 1].to_broadcast([P, GQ_DIM]), c("ident"), start=True, stop=True)
                if h in (1, 5, 9):
                    mm.then_inc(qk_spread, 1)
            for g in range(4):
                f_s = probs[g % 2]
                pe.wait_ge(f_feat_copied, g + 1)
                if g:
                    pe.wait_ge(f_seq_copied, g)
                for n in range(NT):
                    pe.matmul(rot[2][:, 0, :], f_s[:, n, 0:P], dft_cos[:, n, :], start=n == 0, stop=False)
                    mm = pe.matmul(rot[2][:, 0, :], f_s[:, n, P:2 * P], dft_sin[:, n, :], start=False, stop=n == NT - 1)
                mm.then_inc(f_seq, 1)
                if g < 3:
                    feature_sums(g + 1)
                    pe.wait_ge(qk_normed, g + 1)
                    if g:
                        pe.wait_ge(qk_done, g)
                    dst = stat_bank[:, 0, :] if g == 0 else stat_bank[:]
                    pe.matmul(dst, c("rotate"), qk[g], start=True, stop=True).then_inc(qk_rotated, 1)
                part("gqa", 0, ks=(2 * g, 2 * g + 2))
                pe.wait_ge(f_seq_copied, g + 1)
                if g:
                    pe.wait_ge(f_split, g)
                else:
                    pe.wait_ge(v_copied, 1)
                pe.matmul(acc[3][:, 1, :], f_w[:, g, :], probs_t[g % 2][:, 0, :], start=True, stop=True).then_inc(f_out, 1)
            pe.wait_ge(f_split, 4)
            attention("gqa")
            residual("w_out", lambda k: [(f_split, 4)] if k == 0 else [(a_split, UNIT0["gqa"] + 2 * (k - 3))] if k >= 4 else [])
            gate_up(1, "ffn2")
            down(1)

            for j in range(COUNT["conv_in"]):
                square_tile(FIRST["conv_in"] + j, rotating("conv_in", j), xn_hi, xn_lo, ready=operand("mix0") if j == 0 else None,
                            beside={1: {5: lambda: spread_factor("mix0")}, 2: {5: lambda: spread_diagonal(SUM["mix0"] + 2, 0)}}.get(j, {}))
                if j == 0:
                    sums("mix0")
            residual("conv_out", lambda k: [(y_split, k // 2 + 1)])

            def memory_attention(layer):
                kind = f"mem{layer}"
                first = PARTS[kind].index(("q", 0))
                for j in range(AHEAD[kind]):
                    part(kind, j, ready=operand(kind) if j == first else None, beside=norm(kind).get(j, {}))
                attention(kind)
                residual(f"mem_o{layer}", lambda k: [(a_split, UNIT0[kind] + k // 2 + 1)])

            memory_attention(0)
            gate_up(2, "ffn0")
            down(2)

            for j in range(AHEAD["moba"]):
                part("moba", j, ready={0: operand("kv"), 2: operand("mix1")}.get(j),
                     beside={**norm("mix1"), 3: {2: lambda: rotate_group("k", 0), 6: lambda: rotate_group("k", 1)},
                             4: {2: lambda: rotate_group("q", 0), 6: lambda: rotate_group("q", 1)}}.get(j, {}))
            attention("moba")
            residual("moba_o", lambda k: [(a_split, UNIT0["moba"] + k + 1)])
            memory_attention(1)
            gate_up(3, "ffn1")
            down(3)
            sums("final")
            spread_factor("final")

        @block.scalar
        def _(act):
            act.dma_start(vec[:], vectors).then_inc(vec_landed, 16)
            for b in range(KP):
                act.dma_start(x[:, pair(b), :], x_t[:, pair(b), :]).then_inc(x_landed[b], 16)

            def split(t, slot=None, turn=None):
                if slot is None:
                    if t >= TILES:
                        return
                    slot, turn = t % RING, t // RING
                act.wait_ge(landed[slot], 16 * (turn if slot < 2 else turn + 1))
                if not isinstance(t, int) or t >= RING:
                    act.wait_ge(tile_done, t - (RING - 1))
                act.activation(w_hi[slot][:], raw[slot][:], ACT.Copy).then_inc(weight_hi, 1)

            def after(t):
                split(t + RING)

            def round_pair(b, src, gain, hi):
                for k in range(2 * b, 2 * b + 2):
                    e = act.activation(hi[:, k, :], src[:, k, :], ACT.Copy, scale=v(gain, k))
                e.then_inc(rounded, 1)

            def square_pair(b, src):
                act.activation(work[:, pair(b), :], src[:, pair(b), :], ACT.Square).then_inc(squared, 1)

            def squares(name, src):
                if SUM[name]:
                    act.wait_ge(summed, SUM[name])
                for b in range(KP):
                    square_pair(b, src)

            def stream(write, gain, name):
                for b in range(KP):
                    act.wait_ge(written, KP * WRITE[write] + b + 1)
                    round_pair(b, x, gain, xn_hi)
                    if write not in DOWNS and b < KP - 1:
                        after(FIRST[write] + b)
                squares(name, x)

            def gate_up(n):
                t0, r0 = FIRST[f"gu{n}"], ROT[f"gu{n}"]

                def tile(t, j, buf, slot, turn):
                    split(t + RING, slot, turn)
                    act.wait_ge(drained, j + (r0 + 1))
                    act.activation(gu_s[buf][:, 0, :], gu_s[buf][:, 0, :], ACT.Silu).then_inc(gated, 1)
                    act.wait_ge(whole, j + (FF * n + 1))
                    act.activation(h_hi[:, j, :], gu_s[buf][:, 0, :], ACT.Copy).then_inc(h_rounded, 1)

                for j in range(PEEL):
                    tile(t0 + j, j, j % 3, (t0 + j) % RING, (t0 + j) // RING + 1)
                if n == 0:
                    act.wait_ge(mem_landed, 16)
                    squares("mem", mem)
                with act.Fori(0, (FF - PEEL) // 3) as i:
                    for q in range(3):
                        t = t0 + PEEL + q
                        tile(3 * i + t, 3 * i + (PEEL + q), (PEEL + q) % 3, t % RING, i + (t // RING + 1))

            def down_splits(n):
                t0 = FIRST[f"down{n}"]
                with act.Fori(0, FF // 2 // 3) as i:
                    for q in range(3):
                        t = t0 + 1 + q
                        split(3 * i + (t + RING), t % RING, i + (t // RING + 1))

            def attention(kind):
                u0, units, scale = UNIT0[kind], plan(kind), SCALE[kind]

                def exponentials(n):
                    u, a = u0 + n, units[n]
                    act.wait_ge(a_max, u + 1)
                    if u >= 2:
                        act.wait_ge(a_turned, u - 1)
                    for t in range(NT):
                        keys = (t + 1) * P if a["causal"] else S
                        e = act.activation(probs[u % 2][:, t, 0:keys], acc[u % 2][:, t, 0:keys], ACT.Exp, scale=scale,
                                           bias=small[:, u % 2, 1, t:t + 1], accum_out=small[:, u % 2, 2, t:t + 1])
                    e.then_inc(a_exp, 1)

                exponentials(0)
                exponentials(1)
                for n, a in enumerate(units):
                    u = u0 + n
                    for j in ended(kind, n, 0):
                        after(FIRST[kind] + j)
                    act.wait_ge(a_turned, u + 1)
                    if u >= 2:
                        act.wait_ge(a_out, u - 1)
                    if a["causal"]:
                        act.activation(probs_t[u % 2][:, 0, :], acc[2][:, 0, :], ACT.Copy)
                        act.activation(probs_t[u % 2][:, 1, P:S], acc[2][:, 1, P:S], ACT.Copy).then_inc(a_turned_copied, 1)
                    else:
                        act.activation(probs_t[u % 2], acc[2][:], ACT.Copy).then_inc(a_turned_copied, 1)
                    if n + 2 < len(units):
                        exponentials(n + 2)
                    for j in ended(kind, n, 1):
                        after(FIRST[kind] + j)
                    act.wait_ge(a_out, u + 1)
                    b0, b1 = a["blocks"]
                    act.activation(h_hi[a["rows"], b0:b1, :], acc[3][a["rows"], 0:b1 - b0, :], ACT.Copy).then_inc(a_rounded, 1)

            def start(i, tile, k0, k1, last):
                act.wait_ge(start_landed[i], 16)
                act.activation(rows_of(w_hi[tile][:], k0, k1), rows_of(raw[tile][:], k0, k1),
                               ACT.Copy).then_inc(weight_hi if last else start_hi, 1)

            act.wait_ge(vec_landed, 16)
            for b in range(KP):
                start(b, 0, 2 * b, 2 * b + 2, b == KP - 1)
                act.wait_ge(x_landed[b], 16)
                round_pair(b, x, "ffn1_norm", xn_hi)
            for i in range(2):
                start(KP + i, 1, i * KB // 2, (i + 1) * KB // 2, i == 1)
            squares("x0", x)
            split(2, 2, 0)
            gate_up(0)
            after(FIRST["down0"])
            for b in range(KP):
                round_pair(b, mem, "norm_memkv0", mn_hi)
            act.wait_ge(trig_ready, 1)
            act.activation(m_sin[:], scratch[0:32, 6, :], ACT.Sin).then_inc(trig_done, 1)
            act.activation(m_cos[:], scratch[0:32, 7, :], ACT.Sin).then_inc(trig_done, 1)
            down_splits(0)
            stream("down0", "mix_norm", "mix")
            for t in range(-1, 2):
                after(FIRST["w_in"] + t)
            for g in range(3):
                act.wait_ge(drained, ROT["w_in"] + g + 1)
                src = gk_t if g == 0 else q_t[:, 2 * g - 2:2 * g, :]
                dst = (work[:, 4, :], work[:, 5:7, :], scratch[:, 6:8, :])[g]
                act.activation(dst, src, ACT.Square).then_inc(qk_squared, 1)
            after(FIRST["w_in"] + 2)
            act.wait_ge(v_turned, 1)
            act.activation(v_s[:, :, 0:P], acc[3][:, 0, :].rearrange("p (t d) -> p t d", t=NT), ACT.Copy).then_inc(v_copied, 1)
            after(FIRST["w_in"] + 3)
            for g in range(4):
                act.wait_ge(f_feat, g + 1)
                if g >= 2:
                    act.wait_ge(f_seq, g - 1)
                act.activation(probs[g % 2], rot[1][:], ACT.Copy).then_inc(f_feat_copied, 1)
                act.wait_ge(f_seq, g + 1)
                if g >= 2:
                    act.wait_ge(f_out, g - 1)
                act.activation(probs_t[g % 2][:, 0, :], rot[2][:, 0, :], ACT.Copy).then_inc(f_seq_copied, 1)
                act.wait_ge(f_out, g + 1)
                act.activation(h_hi[:, g, :], acc[3][:, 1, :], ACT.Identity, bias=v("fnet_b", g)).then_inc(f_rounded, 1)
                if g == 1:
                    after(FIRST["w_in"] + 4)
            after(FIRST["gqa"])
            attention("gqa")
            stream("w_out", "ffn2_norm", "ffn2")
            after(FIRST["gu1"] - 1)
            gate_up(1)
            after(FIRST["down1"])
            down_splits(1)
            stream("down1", "gain2", "mix0")
            after(FIRST["conv_in"] - 1)
            for p in range(KP):
                for j in range(3):
                    after(FIRST["conv_in"] + 3 * p + j)
                act.wait_ge(y_whole, p + 1)
                act.activation(h_hi[:, pair(p), :], tap_s, ACT.Copy).then_inc(y_rounded, 1)
            stream("conv_out", "norm_mem0", "mem0")
            after(FIRST["mem0"] - 1)
            for j in range(AHEAD["mem0"]):
                after(FIRST["mem0"] + j)
            attention("mem0")
            stream("mem_o0", "norm_ffn0", "ffn0")
            after(FIRST["gu2"] - 1)
            gate_up(2)
            after(FIRST["down2"])
            for b in range(KP):
                round_pair(b, mem, "norm_memkv1", mn_hi)
            down_splits(2)
            stream("down2", "kv_norm", "mix1")
            after(FIRST["moba"] - 1)
            for b in range(KP):
                round_pair(b, x, "norm_mix1", h_hi[:, KB:2 * KB, :])
            for j in range(AHEAD["moba"]):
                after(FIRST["moba"] + j)
            attention("moba")
            stream("moba_o", "norm_mem1", "mem1")
            after(FIRST["mem1"] - 1)
            for j in range(AHEAD["mem1"]):
                after(FIRST["mem1"] + j)
            attention("mem1")
            stream("mem_o1", "norm_ffn1", "ffn1")
            after(FIRST["gu3"] - 1)
            gate_up(3)
            for t in range(FIRST["down3"], TILES - RING):
                after(t)
            act.wait_ge(summed, SUM["final"])
            for b in range(KP):
                act.wait_ge(written, KP * WRITE["down3"] + b + 1)
                square_pair(b, x)

        @block.vector
        def _(dve):
            links = [0]

            def link(e):
                links[0] += 1
                e.then_inc(linked, 1)
                dve.wait_ge(linked, links[0])

            def split(t, slot=None):
                if slot is None:
                    if t >= TILES:
                        return
                    slot = t % RING
                dve.wait_ge(weight_hi, t + 1)
                dve.tensor_tensor(w_lo[slot][:], raw[slot][:], w_hi[slot][:].bitcast(F32), ALU.subtract).then_inc(weight_lo, 1)

            def after(t):
                split(t + RING - 1)

            def rest_pair(name, b, src, gain, hi, lo):
                dve.wait_ge(rounded, KP * OPERAND[name] + b + 1)
                for k in range(2 * b, 2 * b + 2):
                    e = dve.scalar_tensor_tensor(lo[:, k, :], src[:, k, :], v(gain, k), hi[:, k, :].bitcast(F32),
                                                 ALU.mult, ALU.subtract)
                e.then_inc(split_done, 1)

            def stream(write, gain, name, scale=1.0):
                for b in range(KP + 1):
                    if b < KP:
                        if write in DOWNS and b < KP - 1:
                            dve.wait_ge(acc_done, (KP - 1) * DOWNS[write] + b + 1)
                        else:
                            dve.wait_ge(tile_done, FIRST[write] + (COUNT[write] if write in DOWNS else b + 1))
                        dve.scalar_tensor_tensor(x[:, pair(b), :], acc[b][:], scale, x[:, pair(b), :],
                                                 ALU.mult, ALU.add).then_inc(written, 1)
                    if b and gain:
                        rest_pair(name, b - 1, x, gain, xn_hi, xn_lo)
                    if write not in DOWNS and b < KP - 1:
                        after(FIRST[write] + b)

            def inverse_root(n, done=None):
                m, y, t = (root[:, i, 0:n] for i in range(3))
                link(dve.tensor_scalar(y.bitcast(I32), m.bitcast(I32), 1, None, ALU.logical_shift_right))
                link(dve.tensor_scalar(y.bitcast(I32), y.bitcast(I32), -1.0, ROOT_GUESS, ALU.mult, ALU.add))
                for step in range(ROOT_STEPS):
                    link(dve.tensor_tensor(t, y, y, ALU.mult))
                    link(dve.scalar_tensor_tensor(t, t, -0.5, m, ALU.mult, ALU.mult))
                    e = dve.scalar_tensor_tensor(y, t, 1.5, y, ALU.add, ALU.mult)
                    if done is not None and step == ROOT_STEPS - 1:
                        e.then_inc(done, 1)
                    else:
                        link(e)

            def on_diagonal(col):
                for t in range(NT):
                    e = dve.tensor_scalar(diag[:, t, :], c("ident"), col[:, t:t + 1], None, ALU.mult)
                e.then_inc(factor, 1)

            def factors(name, col):
                dve.wait_ge(summed, SUM[name] + 1)
                link(dve.tensor_scalar(root[:, 0, 0:NT], stat_bank[:, 0, 0:NT], 1.0 / D, EPS, ALU.mult, ALU.add))
                inverse_root(NT)
                link(dve.tensor_copy(col[:], root[:, 1, 0:NT]))
                on_diagonal(col)

            def spread_to(name, r):
                dve.wait_ge(spread, SUM[name] + (2 if SUM[name] > SUM["mix0"] else 1))
                dve.tensor_copy(r[:], stat_bank[:, 1, :]).then_inc(spread_read, 1)
                dve.wait_ge(spread_read, SUM[name] + 1)

            def gate_up(n, name):
                t0, r0 = FIRST[f"gu{n}"], ROT[f"gu{n}"]

                def scaled(t, buf, block_of):
                    dve.wait_ge(tile_done, t + 1)
                    dve.tensor_tensor(gu_s[buf], rot[block_of][:], both(r_x[:]), ALU.mult).then_inc(drained, 1)

                def multiplied(j, buf):
                    dve.wait_ge(gated, j + (FF * n + 1))
                    dve.tensor_tensor(gu_s[buf][:, 0, :], gu_s[buf][:, 0, :], gu_s[buf][:, 1, :], ALU.mult).then_inc(whole, 1)

                def rest(j, buf, count):
                    dve.wait_ge(h_rounded, count)
                    dve.tensor_tensor(h_lo[:, j, :], gu_s[buf][:, 0, :], h_hi[:, j, :].bitcast(F32), ALU.subtract).then_inc(h_split, 1)

                after(t0)
                factors(name, col_x)
                after(t0 + 1)
                spread_to(name, r_x)
                for j in range(PEEL):
                    scaled(t0 + j, j % 3, (r0 + j) % 3)
                    if j > 1:
                        after(t0 + j)
                    multiplied(j, j % 3)
                    if j:
                        rest(j - 1, (j - 1) % 3, FF * n + j)
                with dve.Fori(0, (FF - PEEL) // 3) as i:
                    for q in range(3):
                        j, t = PEEL + q, t0 + PEEL + q
                        scaled(3 * i + t, j % 3, (r0 + j) % 3)
                        split(3 * i + (t + RING - 1), (t + RING - 1) % RING)
                        multiplied(3 * i + j, j % 3)
                        rest(3 * i + (j - 1), (j - 1) % 3, 3 * i + (FF * n + j))
                rest(FF - 1, (FF - 1) % 3, FF * (n + 1))

            def down_splits(n):
                t0 = FIRST[f"down{n}"]
                with dve.Fori(0, FF // 2 // 3) as i:
                    for q in range(3):
                        t = t0 + 1 + q + RING - 1
                        split(3 * i + t, t % RING)

            def part(kind, j):
                what, i = PARTS[kind][j]
                t, src = FIRST[kind] + j, rot[(ROT[kind] + j) % 3]
                of_memory = kind != "moba" and what != "q"
                dve.wait_ge(tile_done, t + 1)
                if what == "v":
                    col = col_m if of_memory else col_x
                    for n in range(NT):
                        e = dve.tensor_scalar(v_s[:, n, 2 * P * i:2 * P * (i + 1)], src[:, n, :], col[:, n:n + 1], None, ALU.mult)
                else:
                    dst = k_t if what == "k" else q_t
                    e = dve.tensor_tensor(dst[:, pair(i), :], src[:], both((r_m if of_memory else r_x)[:]), ALU.mult)
                e.then_inc(drained, 1)

            def turn_group(what, j):
                g, part_t = ROPES.index((what, j)), k_t if what == "k" else q_t
                head = part_t[0:32, pair(j), :]
                tmp = work[0:32, 0:2, :]
                if g == 0:
                    dve.wait_ge(trig_done, 2)
                dve.wait_ge(rope_rotated, g + 1)
                dve.tensor_tensor(head, head, both(m_cos[:], 2, 32), ALU.mult)
                link(dve.tensor_tensor(tmp, stat_bank[0:32], both(m_sin[:], 2, 32), ALU.mult))
                dve.tensor_tensor(head, head, tmp, ALU.add).then_inc(rope_done, 1)

            def attention(kind):
                u0, units, scale = UNIT0[kind], plan(kind), SCALE[kind]

                def maxima(n):
                    u, a = u0 + n, units[n]
                    top, low = small[:, u % 2, 0, :], small[:, u % 2, 1, :]
                    dve.wait_ge(a_scores, u + 1)
                    if a["causal"]:
                        own = [acc[u % 2][:, t, t * P:(t + 1) * P] for t in range(NT)]
                        dve.tensor_tensor(own[0], own[0], c("causal"), ALU.add)
                        link(dve.tensor_tensor(own[1], own[1], c("causal"), ALU.add))
                        for t in range(NT):
                            e = dve.tensor_reduce(top[:, t:t + 1], acc[u % 2][:, t, 0:(t + 1) * P], AX.X, ALU.max)
                        link(e)
                    else:
                        link(dve.tensor_reduce(top, acc[u % 2][:], AX.X, ALU.max))
                    dve.tensor_scalar(low, top, -scale, None, ALU.mult).then_inc(a_max, 1)

                def normalise(n):
                    u, a = u0 + n, units[n]
                    dve.wait_ge(a_exp, u + 1)
                    link(dve.reciprocal(small[:, u % 2, 3, :], small[:, u % 2, 2, :]))
                    for t in range(NT):
                        keys = (t + 1) * P if a["causal"] else S
                        pr = probs[u % 2][:, t, 0:keys]
                        e = dve.tensor_scalar(pr, pr, small[:, u % 2, 3, t:t + 1], None, ALU.mult)
                    e.then_inc(a_probs, 1)

                def rest(n):
                    u, a = u0 + n, units[n]
                    b0, b1 = a["blocks"]
                    dve.wait_ge(a_rounded, u + 1)
                    dve.tensor_tensor(h_lo[a["rows"], b0:b1, :], acc[3][a["rows"], 0:b1 - b0, :],
                                      h_hi[a["rows"], b0:b1, :].bitcast(F32), ALU.subtract).then_inc(a_split, 1)

                def pieces(n, i):
                    for piece in PIECES[kind].get(n, ([], []))[i]:
                        if piece in ROPES:
                            turn_group(*piece)
                        elif piece[-1] == KB:
                            part(kind, piece[0])
                            after(FIRST[kind] + piece[0])

                maxima(0)
                maxima(1)
                normalise(0)
                for n in range(len(units)):
                    if n:
                        rest(n - 1)
                    if n + 1 < len(units):
                        normalise(n + 1)
                    pieces(n, 0)
                    if n + 2 < len(units):
                        maxima(n + 2)
                    pieces(n, 1)
                rest(len(units) - 1)

            def start(tile, k0, k1, sem_hi, count, sem_lo):
                dve.wait_ge(sem_hi, count)
                dve.tensor_tensor(rows_of(w_lo[tile][:], k0, k1), rows_of(raw[tile][:], k0, k1),
                                  rows_of(w_hi[tile][:], k0, k1).bitcast(F32), ALU.subtract).then_inc(sem_lo, 1)

            dve.wait_ge(vec_landed, 16)
            for b in range(KP):
                start(0, 2 * b, 2 * b + 2, *((start_hi, b + 1, start_lo) if b < KP - 1 else (weight_hi, 1, weight_lo)))
                rest_pair("x0", b, x, "ffn1_norm", xn_hi, xn_lo)
            start(1, 0, KB // 2, start_hi, KP, start_lo)
            start(1, KB // 2, KB, weight_hi, 2, weight_lo)
            a, b = VCOL["final_norm"][0], VCOL["norm_mix0"][0]
            dve.tensor_tensor(gain2[:], vec[:, a:a + KB], vec[:, b:b + KB], ALU.mult)
            dve.tensor_tensor(weigh[:, :, 1], vec[:, a:a + KB], vec[:, a:a + KB], ALU.mult)
            dve.wait_ge(const_landed, CONST_DMAS)
            gate_up(0, "x0")
            after(FIRST["down0"])
            dve.wait_ge(mem_landed, 16)
            factors("mem", col_m)
            for b in range(KP):
                rest_pair("memkv0", b, mem, "norm_memkv0", mn_hi, mn_lo)
            turn, red, quarter = scratch[0:32, 5, :], scratch[0:32, 6, :], scratch[0:32, 7, :]
            freq = con[0:32, CCOL["inv_freq"][0]:CCOL["inv_freq"][1]]
            link(dve.tensor_copy(turn, pos))
            link(dve.tensor_scalar(red, turn, freq, None, ALU.mult))
            link(dve.tensor_scalar(turn, red, 1.0 / TWO_PI, ROUND, ALU.mult, ALU.add))
            link(dve.tensor_scalar(turn, turn, ROUND, None, ALU.subtract))
            for piece in TURN:
                link(dve.scalar_tensor_tensor(red, turn, -piece, red, ALU.mult, ALU.add))
            link(dve.scalar_tensor_tensor(quarter, red, -1.0, red, ALU.mult, ALU.max))
            link(dve.tensor_scalar(red, red, -PI_BELOW, PI_BELOW, ALU.max, ALU.min))
            dve.tensor_scalar(quarter, quarter, -1.0, float(np.pi / 2), ALU.mult, ALU.add).then_inc(trig_ready, 1)
            down_splits(0)
            spread_to("mem", r_m)
            stream("down0", "mix_norm", "mix", 0.5)
            after(FIRST["w_in"] - 1)

            def qkf(j):
                src = rot[(ROT["w_in"] + j) % 3]
                dve.wait_ge(tile_done, FIRST["w_in"] + j + 1)
                if j == 0:
                    dve.tensor_tensor(gk_t, src[:, 0, :], r_x[:], ALU.mult)
                    e = dve.tensor_tensor(gv_t, src[:, 1, :], r_x[:], ALU.mult)
                else:
                    dst = q_t[:, 2 * j - 2:2 * j, :] if j < 3 else work[:, 2 * j - 6:2 * j - 4, :]
                    e = dve.tensor_tensor(dst, src[:], both(r_x[:]), ALU.mult)
                e.then_inc(drained, 1)

            after(FIRST["w_in"])
            factors("mix", col_x)
            after(FIRST["w_in"] + 1)
            spread_to("mix", r_x)
            for j in range(5):
                qkf(j)
                if j == 2:
                    after(FIRST["w_in"] + j)
                    dve.wait_ge(qk_sum, 1)
                    link(dve.tensor_scalar(root[:, 0, :], stat_bank[:, 0, 0:2 * GQ_HEADS], 1.0 / GQ_DIM, EPS, ALU.mult, ALU.add))
                    inverse_root(2 * GQ_HEADS, done=qk_root)
            after(FIRST["w_in"] + 3)

            def head_norm_rope(g):
                n = 1 if g == 0 else 2
                part_t = q_t[:, 5:6, :] if g == 0 else q_t[:, 2 * g - 2:2 * g, :]
                inv = acc[0][:, 1:2, :] if g == 0 else acc[g][:]
                dve.wait_ge(qk_spread, g + 1)
                dve.scalar_tensor_tensor(part_t, part_t, v("q_norm" if g else "k_norm"), inv, ALU.mult, ALU.mult).then_inc(qk_normed, 1)
                tmp = work[:, 4:4 + n, :]
                dve.wait_ge(qk_rotated, g + 1)
                dve.tensor_tensor(part_t, part_t, both(c("axial_cos"), n), ALU.mult)
                link(dve.tensor_tensor(tmp, stat_bank[:, 0:n, :], both(c("axial_sin"), n), ALU.mult))
                dve.tensor_tensor(part_t, part_t, tmp, ALU.add).then_inc(qk_done, 1)

            for g in range(4):
                if g < 3:
                    head_norm_rope(g)
                dve.wait_ge(f_rounded, g + 1)
                dve.scalar_tensor_tensor(h_lo[:, g, :], acc[3][:, 1, :], v("fnet_b", g), h_hi[:, g, :].bitcast(F32),
                                         ALU.add, ALU.subtract).then_inc(f_split, 1)
                if g == 2:
                    after(FIRST["w_in"] + 4)
            part("gqa", 0)
            after(FIRST["gqa"])
            attention("gqa")
            stream("w_out", "ffn2_norm", "ffn2")
            after(FIRST["gu1"] - 1)
            gate_up(1, "ffn2")
            after(FIRST["down1"])
            down_splits(1)
            stream("down1", "gain2", "mix0", 0.5)
            after(FIRST["conv_in"] - 1)

            dve.wait_ge(summed, SUM["mix0"] + 1)
            sq = stat_bank[:, 0, 0:2 * NT].rearrange("p (t w) -> p t w", w=2)
            link(dve.tensor_scalar(root[:, 0, 0:NT], sq[:, :, 0], 1.0 / D, EPS, ALU.mult, ALU.add))
            link(dve.tensor_scalar(root[:, 2, 0:NT], root[:, 0, 0:NT], EPS, None, ALU.mult))
            link(dve.scalar_tensor_tensor(root[:, 0, NT:2 * NT], sq[:, :, 1], 1.0 / D, root[:, 2, 0:NT], ALU.mult, ALU.add))
            inverse_root(2 * NT)
            dve.tensor_copy(col_1[:], root[:, 1, 0:NT])
            link(dve.tensor_copy(col_x[:], root[:, 1, NT:2 * NT]))
            on_diagonal(col_x)
            after(FIRST["conv_in"])
            dve.wait_ge(spread, SUM["mix0"] + 1)
            link(dve.tensor_copy(r_x[:], stat_bank[:, 1, :]))
            on_diagonal(col_1)
            dve.wait_ge(pads_set, 1)
            for p in range(KP):
                for m in range(2):
                    k, j = 2 * p + m, 3 * p + m
                    dve.wait_ge(tile_done, FIRST["conv_in"] + j + 1)
                    dve.tensor_tensor(conv_s[0], rot[(ROT["conv_in"] + j) % 3][:], both(r_x[:]), ALU.mult).then_inc(drained, 1)
                    if j:
                        after(FIRST["conv_in"] + j)
                    dve.wait_ge(drained, ROT["conv_in"] + j + 1)
                    z, tap = z_s[:, m, :], tap_s[:, m, :]
                    if m == 0 and p:
                        dve.wait_ge(y_split, p)
                    link(dve.tensor_tensor(z[:, 2:S + 2], conv_s[0][:, 0, :], conv_s[0][:, 1, :], ALU.mult))
                    link(dve.tensor_scalar(tap, z[:, 2:S + 2], v("conv_w", 2 * KB + k), None, ALU.mult))
                    for w in (1, 0):
                        link(dve.scalar_tensor_tensor(tap, z[:, w:S + w], v("conv_w", w * KB + k), tap, ALU.mult, ALU.add))
                j = 3 * p + 2
                dve.wait_ge(tile_done, FIRST["conv_in"] + j + 1)
                dve.tensor_tensor(conv_s[1], rot[(ROT["conv_in"] + j) % 3][:], both(r_x[:]), ALU.mult).then_inc(drained, 1)
                after(FIRST["conv_in"] + j)
                dve.wait_ge(drained, ROT["conv_in"] + j + 1)
                dve.tensor_tensor(tap_s, tap_s, conv_s[1], ALU.mult).then_inc(y_whole, 1)
                dve.wait_ge(y_rounded, p + 1)
                dve.tensor_tensor(h_lo[:, pair(p), :], tap_s, h_hi[:, pair(p), :].bitcast(F32), ALU.subtract).then_inc(y_split, 1)
                if p == 0:
                    dve.wait_ge(spread, SUM["mix0"] + 2)
                    for k in range(KB):
                        e = dve.scalar_tensor_tensor(x[:, k, :], x[:, k, :], v("final_norm", k), stat_bank[:, 0, :], ALU.mult, ALU.mult)
                    e.then_inc(spread_read, 1)
            stream("conv_out", "norm_mem0", "mem0")
            after(FIRST["mem0"] - 1)

            def memory_attention(kind):
                part(kind, 0)
                after(FIRST[kind])
                factors(kind, col_x)
                after(FIRST[kind] + 1)
                spread_to(kind, r_x)
                for j in range(1, AHEAD[kind]):
                    part(kind, j)
                    if j > 1:
                        after(FIRST[kind] + j)
                attention(kind)

            memory_attention("mem0")
            stream("mem_o0", "norm_ffn0", "ffn0")
            after(FIRST["gu2"] - 1)
            gate_up(2, "ffn0")
            after(FIRST["down2"])
            for b in range(KP):
                rest_pair("memkv1", b, mem, "norm_memkv1", mn_hi, mn_lo)
            down_splits(2)
            stream("down2", "kv_norm", "kv")
            after(FIRST["moba"] - 1)

            for b in range(KP):
                rest_pair("mix1", b, x, "norm_mix1", h_hi[:, KB:2 * KB, :], h_lo[:, KB:2 * KB, :])
            after(FIRST["moba"])
            factors("mix1", col_x)
            after(FIRST["moba"] + 1)
            spread_to("mix1", r_x)
            for j in range(AHEAD["moba"]):
                part("moba", j)
                if j > 1:
                    after(FIRST["moba"] + j)
                if j in (2, 3):
                    turn_group("kq"[j - 2], 0)
                    turn_group("kq"[j - 2], 1)
            attention("moba")
            stream("moba_o", "norm_mem1", "mem1")
            after(FIRST["mem1"] - 1)
            memory_attention("mem1")
            stream("mem_o1", "norm_ffn1", "ffn1")
            after(FIRST["gu3"] - 1)
            gate_up(3, "ffn1")
            for t in range(FIRST["down3"], TILES - RING + 1):
                after(t)
            stream("down3", None, "final")
            factors("final", col_x)
            dve.wait_ge(spread, SUM["final"] + 2)
            for b in range(KP):
                for k in range(2 * b, 2 * b + 2):
                    e = dve.scalar_tensor_tensor(work[:, k, :], x[:, k, :], v("norm_final", k), stat_bank[:, 1, :], ALU.mult, ALU.mult)
                e.then_inc(out_ready, 1)


def column_blocks(w):
    n = w.shape[1] // (2 * P)
    return w.reshape(KB, P, n, 2, P).transpose(2, 1, 3, 0, 4).reshape(n, P, TILE, P)


def row_blocks(w):
    n = w.shape[0] // (2 * P)
    return w.reshape(n, 2, P, KB, P).transpose(0, 2, 1, 3, 4).reshape(n, P, TILE, P)


def gate_up_blocks(gate, up):
    pad = FF * P - gate.shape[1]
    both = [np.pad(a, ((0, 0), (0, pad))).reshape(D, FF, 1, P) for a in (gate, up)]
    return column_blocks(np.concatenate(both, axis=2).reshape(D, 2 * FF * P))


def down_blocks(w):
    return row_blocks(np.pad(w, ((0, FF * P - w.shape[0]), (0, 0))))


def feature_major(a):
    return np.ascontiguousarray(a.T.reshape(KB, P, a.shape[0]).transpose(1, 0, 2))


def constants():
    def dft(n):
        a = 2 * np.pi * (np.outer(np.arange(n), np.arange(n)) % n) / n
        return np.cos(a), np.sin(a)

    cf, sf = dft(P)
    cs, ss = dft(S)
    ortho = 1.0 / np.sqrt(S * P)
    by_tile = lambda a: a.reshape(NT, P, S).transpose(1, 0, 2).reshape(P, NT * S)
    rotate = np.zeros((P, P))
    i = np.arange(P)
    low = i[i % 32 < 16]
    rotate[low + 16, low] = -1.0
    rotate[low, low + 16] = 1.0
    grid_w, axis_dim = 64, GQ_DIM // 2
    inv = (10000.0 ** (-np.arange(0, axis_dim, 2) / axis_dim)).astype(np.float32)
    tok = np.arange(S)
    place = np.where((i % GQ_DIM < axis_dim)[:, None], (tok // grid_w)[None], (tok % grid_w)[None]).astype(np.float32)
    ang = (place * inv[i % 16][:, None]).astype(np.float32).astype(np.float64)
    freq = np.zeros((P, 1))
    freq[:32, 0] = 500000.0 ** (-2.0 * (np.arange(32) % 16) / 32)
    table = dict(
        dft_feature=np.concatenate([cf, sf], 1), dft_cos=by_tile(cs * ortho), dft_sin=by_tile(-ss * ortho), rotate=rotate,
        head_ones=(i[:, None] // GQ_DIM == np.arange(2)[None]), ident=np.eye(P), axial_cos=np.cos(ang), axial_sin=np.sin(ang),
        causal=np.where(i[:, None] >= i[None], 0.0, -1e30), inv_freq=freq)
    return [np.concatenate([np.asarray(table[n], np.float32) for n, _ in names], axis=1) for names in (CONSTS, FOURIER)]


def kernel(**inputs):
    import concourse.bacc as bacc
    from concourse.bass_utils import run_bass_kernel_spmd

    a = {n: np.asarray(t) for n, t in inputs.items()}
    heads = [h for b in range(4) for h in (b, b + 4)]
    head_cols = np.concatenate([np.arange(h * GQ_DIM, (h + 1) * GQ_DIM) for h in heads])
    f, q, k, val = np.split(a["w_in"], [512, 1024, 1152], axis=1)
    w_in = np.concatenate([k, val, q[:, head_cols], f], axis=1)
    w_out = np.concatenate([a["w_out"][:512], a["w_out"][512:][head_cols]], axis=0)
    gate_b, gate_c, u = (t.reshape(D, KP, 2, 1, P) for t in np.split(a["conv_w_in_2"][0], 3, axis=1))
    conv_in = np.concatenate([np.concatenate([gate_c, u], 3).reshape(D, KP, 4, P), gate_b.reshape(D, KP, 2, P)], 2).reshape(D, 3 * D)
    gu2 = [np.split(w, 2, axis=1) for w in a["ffn_w_gu_2"]]
    mem_kv = [column_blocks(w) for w in a["mem_w_kv_2"]]
    tiles = {
        "gu0": gate_up_blocks(a["ffn1_w_gate"], a["ffn1_w_up"]), "down0": down_blocks(a["ffn1_w_down"]),
        "gu1": gate_up_blocks(a["ffn2_w_gate"], a["ffn2_w_up"]), "down1": down_blocks(a["ffn2_w_down"]),
        "gu2": gate_up_blocks(*gu2[0]), "down2": down_blocks(a["ffn_w_down_2"][0]),
        "gu3": gate_up_blocks(*gu2[1]), "down3": down_blocks(a["ffn_w_down_2"][1]),
        "w_in": column_blocks(w_in), "w_out": column_blocks(w_out),
        "conv_in": column_blocks(conv_in), "conv_out": column_blocks(a["conv_w_out_2"][0]),
        "mem_o0": column_blocks(a["mem_w_o_2"][0]), "mem_o1": column_blocks(a["mem_w_o_2"][1]),
        "moba_o": column_blocks(a["moba_w_o_2"][0]),
    }
    key, value = slice(0, KP), slice(KP, 2 * KP)
    moba_kv = column_blocks(a["w_kv_2"])
    sources = {
        "gqa": {"k": mem_kv[0][key]},
        "mem0": {"q": column_blocks(a["mem_w_q_2"][0]), "v": mem_kv[0][value]},
        "moba": {"k": moba_kv[key], "q": column_blocks(a["moba_w_q_2"][0]), "v": moba_kv[value]},
        "mem1": {"k": mem_kv[1][key], "q": column_blocks(a["mem_w_q_2"][1]), "v": mem_kv[1][value]},
    }
    for kind, parts in PARTS.items():
        tiles[kind] = np.stack([sources[kind][what][i] for what, i in parts])
    weights = np.concatenate([tiles[n] for n, _ in STREAM], axis=0)
    by_block = lambda t: t.reshape(-1, P).T
    vec = {
        "ffn1_norm": a["ffn1_norm"], "mix_norm": a["mix_norm"], "ffn2_norm": a["ffn2_norm"], "final_norm": a["final_norm"],
        "norm_mix0": a["norm_mix_2"][0], "norm_mix1": a["norm_mix_2"][1], "norm_mem0": a["norm_mem_2"][0],
        "norm_mem1": a["norm_mem_2"][1], "norm_memkv0": a["norm_memkv_2"][0], "norm_memkv1": a["norm_memkv_2"][1],
        "norm_ffn0": a["norm_ffn_2"][0], "norm_ffn1": a["norm_ffn_2"][1], "norm_final": a["norm_final_2"],
        "kv_norm": a["kv_norm_2"], "conv_w": a["conv_w_2"][0], "fnet_b": a["fnet_b"],
        "q_norm": np.concatenate([a["q_norm"]] * 2), "k_norm": np.concatenate([a["k_norm"]] * 2),
    }
    consts, fourier = constants()
    arrays = {
        "weights": weights, "x_t": feature_major(a["x"][0]), "mem_t": feature_major(a["mem_2"][0]),
        "vectors": np.ascontiguousarray(np.concatenate([by_block(vec[n]) for n, _ in VECTORS], axis=1)),
        "consts": consts, "fourier": fourier,
        "fnet_w": np.ascontiguousarray(a["fnet_w"].transpose(1, 0, 2)),
        "positions": np.ascontiguousarray(np.broadcast_to(a["positions_2"].astype(np.int32), (32, S))),
    }
    nc = bacc.Bacc("TRN2", target_bir_lowering=False, num_devices=1, dynamic_dma_scratch_size=1024)
    args = [nc.dram_tensor(n, t.shape, mybir.dt.from_np(t.dtype), kind="ExternalInput").ap() for n, t in arrays.items()]
    args.append(nc.dram_tensor("out_t", (P, KB, S), F32, kind="ExternalOutput").ap())
    program(nc, *args)
    r = run_bass_kernel_spmd(nc, [arrays], core_ids=[0])
    out = r.results[0]["out_t"]
    return np.ascontiguousarray(out.transpose(1, 0, 2).reshape(D, S).T)[None]
```

```python
from contextlib import ExitStack

import numpy as np
import concourse.bass as bass
from concourse import mybir

F32 = mybir.dt.float32
F32R = mybir.dt.float32r
I32 = mybir.dt.int32
ALU = mybir.AluOpType
ACT = mybir.ActivationFunctionType
AX = mybir.AxisListType

P = 128
S = 256
D = 1024
KB = D // P
KP = KB // 2
NT = S // P
TILE = 16
RING = 3
HIDDEN1, HIDDEN2 = 2752, 2816
FF = HIDDEN2 // P
LAST = HIDDEN1 % P
PEEL = 4
EPS = 1e-6
GQ_DIM, MEM_DIM, MOBA_DIM = 64, 256, 128
GQ_HEADS = 10

MEM0 = [("v", 0), ("q", 0), ("q", 1), ("q", 2), ("q", 3), ("v", 1), ("v", 2), ("v", 3)]
MOBA = [("k", 0), ("k", 1), ("v", 0), ("q", 0), ("q", 1), ("k", 2), ("q", 2), ("v", 1), ("k", 3), ("q", 3), ("v", 2), ("v", 3),
        ("m", 0), ("m", 1)]
MEM1 = [("q", 0), ("q", 1), ("v", 0), ("k", 2), ("q", 2), ("k", 3), ("q", 3), ("v", 1), ("v", 2), ("v", 3)]
GQA = [("k", j) for j in range(KP)]
PARTS = {"gqa": GQA, "mem0": MEM0, "moba": MOBA, "mem1": MEM1}
STREAM = [
    ("gu0", FF), ("down0", FF // 2), ("w_in", 5), ("gqa", len(GQA)), ("w_out", KP),
    ("gu1", FF), ("down1", FF // 2), ("conv_in", 12), ("conv_out", KP),
    ("mem0", len(MEM0)), ("mem_o0", KP), ("gu2", FF), ("down2", FF // 2),
    ("moba", len(MOBA)), ("moba_o", KP), ("mem1", len(MEM1)), ("mem_o1", KP), ("gu3", FF), ("down3", FF // 2),
]
WRITES = ["down0", "w_out", "down1", "conv_out", "mem_o0", "down2", "moba_o", "mem_o1", "down3"]
WRITE = {n: i for i, n in enumerate(WRITES)}
DOWNS = {n: i for i, n in enumerate([w for w in WRITES if w.startswith("down")])}
FIRST, COUNT, ROT = {}, {}, {}
_t = _r = 0
for _name, _n in STREAM:
    FIRST[_name], COUNT[_name], ROT[_name] = _t, _n, _r
    _t += _n
    _r += 0 if _name in WRITE else _n
TILES = _t

AHEAD = {"gqa": 1, "mem0": 4, "moba": 5, "mem1": 3}
PIECES = {
    "gqa": {0: ([(1, 0, 3)], [(1, 3, 6)]), 1: ([], [(1, 6, 8), (2, 0, 1)]), 2: ([], [(2, 1, 4)]), 3: ([], [(2, 4, 7)]),
            4: ([], [(2, 7, 8), (3, 0, 2)]), 5: ([], [(3, 2, 4)]), 6: ([], [(3, 4, 6)]), 7: ([], [(3, 6, 8)])},
    "mem0": {0: ([(4, 0, 4)], [(4, 4, 8), (5, 0, 4)]), 1: ([], [(5, 4, 8), (6, 0, 4)]), 2: ([], [(6, 4, 8), (7, 0, 5)]),
             3: ([(7, 5, 8)], [])},
    "moba": {0: ([(5, 0, 8)], [(6, 0, 8)]), 1: ([], [(7, 0, 8)]), 2: ([], [(8, 0, 8)]), 3: ([], [(9, 0, 8), (10, 0, 6)]),
             4: ([], [(10, 6, 8), (11, 0, 5)]), 5: ([], [(11, 5, 8), (12, 0, 5)]), 6: ([], [(12, 5, 8), (13, 0, 4)]),
             7: ([], [(13, 4, 8)])},
    "mem1": {0: ([(3, 0, 8), (4, 0, 8), (5, 0, 2)], [(5, 2, 8), (6, 0, 8)]), 1: ([], [(7, 0, 8), (8, 0, 3)]),
             2: ([], [(8, 3, 8), (9, 0, 4)]), 3: ([(9, 4, 8)], [])},
}
ROPES = [("k", 0), ("q", 0), ("k", 1), ("q", 1), ("k", 2), ("q", 2), ("k", 3), ("q", 3)]

VECTORS = [("ffn1_norm", KB), ("mix_norm", KB), ("ffn2_norm", KB), ("final_norm", KB), ("norm_mix0", KB),
           ("norm_mix1", KB), ("norm_mem0", KB), ("norm_mem1", KB), ("norm_memkv0", KB), ("norm_memkv1", KB),
           ("norm_ffn0", KB), ("norm_ffn1", KB), ("norm_final", KB), ("kv_norm", KB), ("conv_w", 3 * KB),
           ("fnet_b", 4), ("q_norm", 1), ("k_norm", 1)]
CONSTS = [("head_ones", 2), ("ident", P), ("axial_cos", S), ("axial_sin", S), ("causal", P), ("inv_freq", 1)]
FOURIER = [("dft_feature", 2 * P), ("dft_cos", NT * S), ("dft_sin", NT * S)]


def columns(table):
    at, out = 0, {}
    for name, n in table:
        out[name] = (at, at + n)
        at += n
    return out, at


VCOL, NV = columns(VECTORS)
CCOL, NC = columns(CONSTS)
FCOL, _ = columns(FOURIER)

SUMS = ["x0", "mem", "mix", "ffn2", "mix0", "mem0", "ffn0", "mix1", "mem1", "ffn1", "final"]
SUM = {n: i for i, n in enumerate(SUMS)}
FOLDED = [n for n in SUMS if n not in ("mix0", "final")]
FOLD = {n: i for i, n in enumerate(FOLDED)}
OPERANDS = ["x0", "memkv0", "mix", "ffn2", "mix0", "mem0", "ffn0", "memkv1", "kv", "mix1", "mem1", "ffn1"]
OPERAND = {n: i for i, n in enumerate(OPERANDS)}

GQ_UNITS = [(b, half) for b in range(4) for half in range(2)]
UNITS = {"gqa": 8, "mem0": 4, "moba": 8, "mem1": 4}
UNIT0 = {"gqa": 0, "mem0": 8, "moba": 12, "mem1": 20}
SCALE = {"gqa": GQ_DIM ** -0.5, "mem0": MEM_DIM ** -0.5, "moba": MOBA_DIM ** -0.5, "mem1": MEM_DIM ** -0.5}

TWO_PI = 2 * np.pi
_C1 = 6.28125
_C2 = float(np.round((TWO_PI - _C1) * 2 ** 17) / 2 ** 17)
_C3 = float(np.round((TWO_PI - _C1 - _C2) * 2 ** 26) / 2 ** 26)
TURN = (_C1, _C2, _C3, float(TWO_PI - _C1 - _C2 - _C3))
ROUND = 1.5 * 2 ** 23
HALVES_SWAPPED = [(i + 16) % 32 for i in range(32)]
PI_BELOW = 3.1415925
ROOT_GUESS = float(0x5F3759DF)
ROOT_STEPS = 3


def program(nc, weights, x_t, mem_t, vectors, consts, fourier, fnet_w, positions, out_t):
    ctx = ExitStack()
    with ctx:
        def sb(name, shape, dt=F32):
            return ctx.enter_context(nc.sbuf_tensor(name, shape, dt))

        def sem(name):
            return ctx.enter_context(nc.semaphore(name))

        raw = [sb(f"raw{i}", [P, TILE, P]) for i in range(RING)]
        w_hi = [sb(f"w_hi{i}", [P, TILE, P], F32R) for i in range(RING)]
        w_lo = [sb(f"w_lo{i}", [P, TILE, P], F32R) for i in range(RING)]
        x = sb("x", [P, KB, S])
        mem = sb("mem", [P, KB, S])
        work = sb("work", [P, KB, S])
        xn_hi = sb("xn_hi", [P, KB, S], F32R)
        xn_lo = sb("xn_lo", [P, KB, S], F32R)
        mn_hi = sb("mn_hi", [P, KB, S], F32R)
        mn_lo = sb("mn_lo", [P, KB, S], F32R)
        h_hi = sb("h_hi", [P, FF, S], F32R)
        h_lo = sb("h_lo", [P, FF, S], F32R)
        q_t = sb("q_t", [P, KB, S])
        k_t = sb("k_t", [P, KB, S])
        v_s = sb("v_s", [P, NT, D])
        vec = sb("vec", [P, NV])
        con = sb("con", [P, NC])
        ones = sb("ones", [P, P])
        gain2 = sb("gain2", [P, KB])
        weigh = sb("weigh", [P, KB, 2])
        m_cos = sb("m_cos", [32, S])
        m_sin = sb("m_sin", [32, S])
        pos = m_cos[:].bitcast(I32)
        r_x = sb("r_x", [P, S])
        r_m = sb("r_m", [P, S])
        diag = sb("diag", [P, NT, P])
        scratch = sb("scratch", [P, 8, S])
        small = sb("small", [P, 2, 4, NT])
        root = sb("root", [P, 3, 2 * GQ_HEADS])
        col_x = sb("col_x", [P, NT])
        col_m = sb("col_m", [P, NT])
        col_1 = sb("col_1", [P, NT])
        z_s = sb("z_s", [P, 2, S + 2])

        gu_s = [scratch[:, 2 * i:2 * i + 2, :] for i in range(3)]
        probs = [scratch[:, 2 * i:2 * i + 2, :] for i in range(2)]
        probs_t = [scratch[:, 4 + 2 * i:6 + 2 * i, :] for i in range(2)]
        conv_s = [scratch[:, 0:2, :], scratch[:, 2:4, :]]
        tap_s = scratch[:, 4:6, :]
        gv_t, gk_t, f_w = q_t[:, 4, :], q_t[:, 5, :], q_t[:, 6:8, :].rearrange("p a (b d) -> p (a b) d", d=P)
        dft_feature = v_s[:, 0, 2 * P:4 * P]
        dft_cos = v_s[:, 0, 512:1024].rearrange("p (t s) -> p t s", t=NT)
        dft_sin = v_s[:, 1, 512:1024].rearrange("p (t s) -> p t s", t=NT)

        bank = [ctx.enter_context(nc.psum_tensor(f"bank{i}", [P, 2, S], F32)) for i in range(8)]
        rot = bank[0:3]
        stat_bank = bank[3]
        acc = bank[4:8]

        def v(name, i=0):
            if name == "gain2":
                return gain2[:, i:i + 1]
            a = VCOL[name][0] + i
            return vec[:, a:a + 1]

        def c(name):
            a, b = CCOL[name]
            return con[:, a:b]

        def both(t, n=2, rows=P):
            return t.rearrange("p (o s) -> p o s", o=1).to_broadcast([rows, n, S])

        def rows_of(tile, k0, k1):
            return tile.rearrange("p (m k) c -> p m k c", m=2)[:, :, k0:k1, :]

        def pair(b):
            return slice(2 * b, 2 * b + 2)

        landed = [sem(f"weights_landed{i}") for i in range(RING)]
        start_landed = [sem(f"start_landed{i}") for i in range(KP + 2 * (RING - 1))]
        start_hi, start_lo = sem("start_hi"), sem("start_lo")
        x_landed = [sem(f"x_landed{b}") for b in range(KP)]
        vec_landed, mem_landed, const_landed = sem("vec_landed"), sem("mem_landed"), sem("const_landed")
        fourier_landed = sem("fourier_landed")
        ones_set, pads_set = sem("ones_set"), sem("pads_set")
        weight_hi, weight_lo = sem("weight_hi"), sem("weight_lo")
        tile_done = sem("tile_done")
        drained = sem("drained")
        acc_done = sem("acc_done")
        gated, whole, h_rounded, h_split = sem("gated"), sem("whole"), sem("h_rounded"), sem("h_split")
        written = sem("written")
        rounded, split_done = sem("rounded"), sem("split_done")
        squared, folded, summed = sem("squared"), sem("folded"), sem("summed")
        factor, spread, spread_read = sem("factor"), sem("spread"), sem("spread_read")
        linked = sem("linked")
        trig_ready, trig_done = sem("trig_ready"), sem("trig_done")
        qk_squared, qk_sum, qk_root, qk_spread, qk_normed, qk_done = (
            sem(n) for n in ("qk_squared", "qk_sum", "qk_root", "qk_spread", "qk_normed", "qk_done"))
        v_turned, v_copied = sem("v_turned"), sem("v_copied")
        f_feat, f_feat_copied, f_seq, f_seq_copied, f_out, f_rounded, f_split = (
            sem(n) for n in ("f_feat", "f_feat_copied", "f_seq", "f_seq_copied", "f_out", "f_rounded", "f_split"))
        a_scores, a_max, a_exp, a_probs, a_turned, a_turned_copied, a_out, a_rounded, a_split = (
            sem(n) for n in ("a_scores", "a_max", "a_exp", "a_probs", "a_turned", "a_turned_copied", "a_out",
                             "a_rounded", "a_split"))
        y_whole, y_rounded, y_split = sem("y_whole"), sem("y_rounded"), sem("y_split")
        rope_swapped, rope_scaled, rope_done = sem("rope_swapped"), sem("rope_scaled"), sem("rope_done")
        out_gained, out_ready, stored = sem("out_gained"), sem("out_ready"), sem("stored")

        CONST_DMAS = 2 * 16
        FOURIER_DMAS = 4 * 16

        def plan(kind):
            units = []
            for n in range(UNITS[kind]):
                if kind == "gqa":
                    b, half = GQ_UNITS[n]
                    rows = slice(half * GQ_DIM, (half + 1) * GQ_DIM)
                    units.append(dict(q=[q_t[rows, b, :]], k=[gk_t[rows, :]], v=[v_s[:, :, 0:P]],
                                      rows=rows, blocks=(4 + b, 5 + b), causal=False))
                elif kind == "moba":
                    units.append(dict(q=[q_t[:, n, :]], k=[k_t[:, n, :]], v=[v_s[:, :, n * P:(n + 1) * P]],
                                      rows=slice(0, P), blocks=(n, n + 1), causal=True, v_tile=MOBA.index(("v", n // 2))))
                else:
                    parts = PARTS[kind]
                    units.append(dict(q=[q_t[:, 2 * n + i, :] for i in range(2)],
                                      k=[k_t[:, 2 * n + i, :] for i in range(2)],
                                      v=[v_s[:, :, (2 * n + i) * P:(2 * n + i + 1) * P] for i in range(2)],
                                      rows=slice(0, P), blocks=(2 * n, 2 * n + 2), causal=False,
                                      qk_tile=max(parts.index(p) for p in (("q", n), ("k", n)) if p in parts),
                                      v_tile=parts.index(("v", n))))
            return units

        def rope_partner(g):
            return work[0:32, g % 2 * 2:g % 2 * 2 + 2, :]

        def turns(n):
            return (FF - PEEL) // 3 - (1 if n < 2 else 0)

        def ended(kind, n, i):
            return [piece[0] for piece in PIECES[kind].get(n, ([], []))[i] if piece[-1] == KB]

        block = ctx.enter_context(nc.Block())

        @block.sync
        def _(sp):
            for b in range(KP):
                sp.dma_start(rows_of(raw[0][:], 2 * b, 2 * b + 2), rows_of(weights[0], 2 * b, 2 * b + 2)).then_inc(start_landed[b], 16)
                sp.dma_start(x[:, pair(b), :], x_t[:, pair(b), :]).then_inc(x_landed[b], 16)
            for i in range(2 * (RING - 1)):
                t, a, b = 1 + i // 2, i % 2 * KB // 2, (i % 2 + 1) * KB // 2
                sp.dma_start(rows_of(raw[t][:], a, b), rows_of(weights[t], a, b)).then_inc(start_landed[KP + i], 16)
            sp.dma_start(con[:], consts).then_inc(const_landed, 16)
            sp.dma_start(pos, positions).then_inc(const_landed, 16)
            for s in range(RING):
                sp.wait_ge(weight_lo, s + 1)
                sp.dma_start(raw[s][:], weights[RING + s]).then_inc(landed[s], 16)
            sp.dma_start(mem[:], mem_t).then_inc(mem_landed, 16)
            with sp.Fori(2, 4) as i:
                for s in range(RING):
                    sp.wait_ge(weight_lo, RING * i + s - RING + 1)
                    sp.dma_start(raw[s][:], weights[RING * i + s]).then_inc(landed[s], 16)
            for name, dst in (("dft_feature", v_s[:, 0, 256:512]), ("dft_cos", v_s[:, 0, 512:1024]),
                              ("dft_sin", v_s[:, 1, 512:1024])):
                a, b = FCOL[name]
                sp.dma_start(dst, fourier[:, a:b]).then_inc(fourier_landed, 16)
            sp.dma_start(f_w, fnet_w).then_inc(fourier_landed, 16)
            with sp.Fori(4, TILES // RING) as i:
                for s in range(RING):
                    sp.wait_ge(weight_lo, RING * i + s - RING + 1)
                    sp.dma_start(raw[s][:], weights[RING * i + s]).then_inc(landed[s], 16)
            for t in range(TILES // RING * RING, TILES):
                sp.wait_ge(weight_lo, t - RING + 1)
                sp.dma_start(raw[t % RING][:], weights[t]).then_inc(landed[t % RING], 16)
            for b in range(KP):
                sp.wait_ge(out_ready, b + 1)
                sp.dma_start(out_t[:, pair(b), :], work[:, pair(b), :]).then_inc(stored, 16)
            sp.wait_ge(stored, 16 * KP)

        @block.gpsimd
        def _(pool):
            pool.memset(ones[:], 1.0).then_inc(ones_set, 1)
            pool.memset(weigh[:, :, 0:1], 1.0).then_inc(ones_set, 1)
            pool.memset(z_s[:, :, 0:2], 0.0).then_inc(pads_set, 1)
            def block_rope():
                pool.wait_ge(trig_done, 2)
                for g, (what, j) in enumerate(ROPES):
                    head, partner = (q_t if what == "q" else k_t)[0:32, pair(j), :], rope_partner(g)
                    pool.wait_ge(rope_swapped, g + 1)
                    pool.tensor_tensor(head, head, both(m_cos[:], 2, 32), ALU.mult).then_inc(rope_scaled, 1)
                    pool.tensor_tensor(partner, partner, both(m_sin[:], 2, 32), ALU.mult).then_inc(rope_scaled, 1)
                    pool.wait_ge(rope_scaled, 2 * g + 2)
                    pool.tensor_tensor(head, head, partner, ALU.add).then_inc(rope_done, 1)

            for i, name in enumerate(FOLDED):
                for b in range(1, KP):
                    pool.wait_ge(squared, KP * SUM[name] + b + 1)
                    if b > 1:
                        pool.wait_ge(folded, KP * i + b - 1)
                    pool.tensor_tensor(work[:, 0:2, :], work[:, 0:2, :], work[:, pair(b), :], ALU.add).then_inc(folded, 1)
                pool.wait_ge(folded, KP * (i + 1) - 1)
                pool.tensor_tensor(work[:, 0, :], work[:, 0, :], work[:, 1, :], ALU.add).then_inc(folded, 1)
                if name == "mix1":
                    block_rope()

        @block.tensor
        def _(pe):
            def products(out, hi, lo, rhs_hi, rhs_lo, first, last):
                pe.matmul(out, hi, rhs_hi, start=first, stop=False, skip_group_check=True)
                pe.matmul(out, hi, rhs_lo, start=False, stop=False, skip_group_check=True)
                return pe.matmul(out, lo, rhs_hi, start=False, stop=last, skip_group_check=True)

            def square_tile(t, out, a_hi, a_lo, slot=None, ready=None, beside={}, in_parts=False, ks=(0, KB), ms=2):
                slot = t % RING if slot is None else slot
                if ks[0] == 0 and not in_parts:
                    pe.wait_ge(weight_lo, t + 1)
                for k in range(*ks):
                    if ready is not None:
                        for s, value in ready(k):
                            pe.wait_ge(s, value)
                    if k in beside:
                        beside[k]()
                    for m in range(ms):
                        mm = products(out[:, m, :], w_hi[slot][:, m * KB + k, :], w_lo[slot][:, m * KB + k, :],
                                      a_hi[:, k, :], a_lo[:, k, :], k == 0 and m == 0, k == KB - 1)
                if ks[1] == KB:
                    mm.then_inc(tile_done, 1)

            def value_tile(t, out, a_hi, a_lo, beside={}, ks=(0, KB)):
                wh, wl = (w[t % RING][:].rearrange("p (m k) c -> p k m c", m=2) for w in (w_hi, w_lo))
                if ks[0] == 0:
                    pe.wait_ge(weight_lo, t + 1)
                for k in range(*ks):
                    if k in beside:
                        beside[k]()
                    for n in range(NT):
                        o = out[:, n, :].rearrange("p (m c) -> p m c", m=2)
                        mm = products(o, a_hi[:, k, n * P:(n + 1) * P], a_lo[:, k, n * P:(n + 1) * P],
                                      wh[:, k], wl[:, k], k == 0 and n == 0, k == KB - 1)
                if ks[1] == KB:
                    mm.then_inc(tile_done, 1)

            def operand(name):
                return lambda k: [(split_done, KP * OPERAND[name] + k // 2 + 1)] if k % 2 == 0 else []

            def rotating(name, j, fresh=True):
                r = ROT[name] + j
                if r >= 3 and fresh:
                    pe.wait_ge(drained, r - 2)
                return rot[r % 3]

            def sums(name, ks=None):
                pe.wait_ge(ones_set, 2)
                if SUM[name]:
                    pe.wait_ge(spread_read, SUM[name])
                blocks, cols = (1, 1) if name in FOLD else (KB, 2) if name == "mix0" else (KB, 1)
                if name in FOLD:
                    pe.wait_ge(folded, KP * (FOLD[name] + 1))
                for k in range(*(ks or (0, blocks))):
                    if name not in FOLD and k % 2 == 0:
                        pe.wait_ge(squared, KP * SUM[name] + k // 2 + 1)
                    for n in range(NT):
                        mm = pe.matmul(stat_bank[:, 0, cols * n:cols * (n + 1)], work[:, k, n * P:(n + 1) * P],
                                       weigh[:, k, 0:cols], start=k == 0 and n == 0, stop=k == blocks - 1,
                                       skip_group_check=True)
                if not ks or ks[1] == blocks:
                    mm.then_inc(summed, 1)

            def spread_diagonal(count, half):
                pe.wait_ge(factor, count)
                for t in range(NT):
                    mm = pe.matmul(stat_bank[:, half, t * P:(t + 1) * P], ones[:], diag[:, t, :], start=True, stop=True)
                mm.then_inc(spread, 1)

            def spread_factor(name):
                spread_diagonal(SUM[name] + (2 if SUM[name] > SUM["mix0"] else 1), 1)

            def norm(name, late=False):
                return {1: {7 if late else 4: lambda: sums(name)}, 2: {5 if late else 3: lambda: spread_factor(name)}}

            def gate_up(n, name):
                phase = f"gu{n}"
                t0, r0 = FIRST[phase], ROT[phase]
                for j in range(PEEL):
                    ready = operand(name) if j == 0 else None
                    in_parts = n == 0 and j < RING
                    if in_parts and j == 0:
                        ready = lambda k: operand(name)(k) + (
                            [] if k % 2 else [(start_lo, k // 2 + 1)] if k < KB - 2 else [(weight_lo, 1)])
                    elif in_parts:
                        ready = lambda k: {0: [(start_lo, KP - 1 + j)], KB // 2: [(weight_lo, j + 1)]}.get(k, [])
                    square_tile(t0 + j, rotating(phase, j), xn_hi, xn_lo, ready=ready, in_parts=in_parts,
                                beside=norm(name, n == 0).get(j, {}))
                with pe.Fori(0, turns(n)) as i:
                    for q in range(3):
                        pe.wait_ge(drained, 3 * i + (r0 + PEEL + q - 2))
                        square_tile(3 * i + (t0 + PEEL + q), rot[(r0 + PEEL + q) % 3], xn_hi, xn_lo,
                                    slot=(t0 + PEEL + q) % RING)
                for j in range(PEEL + 3 * turns(n), FF):
                    square_tile(t0 + j, rotating(phase, j), xn_hi, xn_lo, ms=1 if j == FF - 1 else 2)

            def down(n, early=None, late=None, beside=None):
                t0 = FIRST[f"down{n}"]
                w = WRITE[f"down{n}"]

                def blocks(slot, row, order, start, stop, beside={}, rows=P):
                    for k, m in order:
                        if (k, m) in beside:
                            beside[k, m]()
                        r = slice(0, rows if k == 1 else P)
                        mm = products(acc[m // 2][:, m % 2, :], w_hi[slot][r, k * KB + m, :], w_lo[slot][r, k * KB + m, :],
                                      h_hi[r, row + k, :], h_lo[r, row + k, :], start and k == 0 and m % 2 == 0, stop and k == 1)
                        if stop and k == 1 and m % 2 and m < KB - 1:
                            mm.then_inc(acc_done, 1)
                    mm.then_inc(tile_done, 1)

                by_row = [(k, m) for k in range(2) for m in range(KB)]
                pe.wait_ge(weight_lo, t0 + 1)
                pe.wait_ge(h_split, FF * n + 2)
                if w:
                    pe.wait_ge(written, KP * w)
                blocks(t0 % RING, 0, by_row, True, False)
                if early:
                    early()
                with pe.Fori(0, FF // 2 // 3) as i:
                    for q in range(3):
                        pe.wait_ge(weight_lo, 3 * i + (t0 + 2 + q))
                        pe.wait_ge(h_split, 6 * i + (FF * n + 2 * (2 + q)))
                        blocks((t0 + 1 + q) % RING, 6 * i + 2 * (1 + q), by_row, False, False)
                if late:
                    late()
                pe.wait_ge(weight_lo, t0 + FF // 2)
                pe.wait_ge(h_split, FF * n + FF)
                blocks((t0 + FF // 2 - 1) % RING, FF - 2, [(k, m) for m in range(KB) for k in range(2)], False, True,
                       beside or {}, LAST if n < 2 else P)

            def residual(name, ready):
                pe.wait_ge(written, KP * WRITE[name])
                for b in range(KP):
                    square_tile(FIRST[name] + b, acc[b], h_hi, h_lo, ready=ready if b == 0 else None)

            def part(kind, j, ks=(0, KB), **more):
                what = PARTS[kind][j][0]
                t, out = FIRST[kind] + j, rotating(kind, j, ks[0] == 0)
                if kind == "moba":
                    queries = (h_hi[:, KB:2 * KB, :], h_lo[:, KB:2 * KB, :])
                    src = {"q": queries, "m": (mn_hi, mn_lo)}.get(what, (xn_hi, xn_lo))
                else:
                    src = (xn_hi, xn_lo) if what == "q" else (mn_hi, mn_lo)
                if what == "v":
                    value_tile(t, out, *src, ks=ks, beside=more.get("beside", {}))
                else:
                    square_tile(t, out, *src, ks=ks, **more)

            def attention(kind):
                u0, units = UNIT0[kind], plan(kind)

                def pieces(n, i):
                    for j, k0, k1 in PIECES[kind].get(n, ([], []))[i]:
                        part(kind, j, ks=(k0, k1))

                def scores(*ns):
                    for n in ns:
                        u, a = u0 + n, units[n]
                        if u >= 2:
                            pe.wait_ge(a_exp, u - 1)
                        if "qk_tile" in a:
                            pe.wait_ge(drained, ROT[kind] + a["qk_tile"] + 1)
                        if kind == "moba":
                            pe.wait_ge(rope_done, ROPES.index(("q", n // 2)) + 1)
                        if kind == "gqa":
                            pe.wait_ge(qk_done, 2 if n < 4 else 3)
                    for t in range(NT):
                        keys = (t + 1) * P if units[ns[0]]["causal"] else S
                        for i in range(len(units[ns[0]]["q"])):
                            for n in ns:
                                a = units[n]
                                mm = pe.matmul(acc[(u0 + n) % 2][:, t, 0:keys], a["q"][i][:, t * P:(t + 1) * P],
                                               a["k"][i][:, 0:keys], start=i == 0, stop=i == len(a["q"]) - 1)
                    mm.then_inc(a_scores, len(ns))

                paired = kind == "gqa"
                if paired:
                    scores(0, 1)
                else:
                    scores(0)
                    scores(1)
                for n, a in enumerate(units):
                    u = u0 + n
                    pieces(n, 0)
                    pe.wait_ge(a_probs, u + 1)
                    if u:
                        pe.wait_ge(a_turned_copied, u)
                    for t in range(NT):
                        for kt in range(t + 1 if a["causal"] else NT):
                            mm = pe.transpose(acc[2][:, kt, t * P:(t + 1) * P], probs[u % 2][:, t, kt * P:(kt + 1) * P],
                                              c("ident"))
                    mm.then_inc(a_turned, 1)
                    if n + 2 < len(units) and not paired:
                        scores(n + 2)
                    elif n + 2 < len(units) and n % 2 == 0:
                        scores(n + 2, n + 3)
                    pieces(n, 1)
                    if "v_tile" in a:
                        pe.wait_ge(drained, ROT[kind] + a["v_tile"] + 1)
                    pe.wait_ge(a_turned_copied, u + 1)
                    if u:
                        pe.wait_ge(a_split, u)
                    else:
                        pe.wait_ge(f_split, 4)
                    for i, val in enumerate(a["v"]):
                        for kt in range(NT):
                            q0 = kt * P if a["causal"] else 0
                            mm = pe.matmul(acc[3][:, i, q0:S], val[:, kt, :], probs_t[u % 2][:, kt, q0:S],
                                           start=kt == 0, stop=kt == NT - 1, skip_group_check=True)
                    mm.then_inc(a_out, 1)

            gate_up(0, "x0")
            down(0, early=lambda: sums("mem"), late=lambda: spread_factor("mem"))
            pe.wait_ge(const_landed, CONST_DMAS)
            qk_sq = [work[:, 4, :], work[:, 5, :], work[:, 6, :], scratch[:, 6, :], scratch[:, 7, :]]

            def head_sums():
                pe.wait_ge(qk_squared, 3)
                for t in range(NT):
                    for b in range(GQ_HEADS // 2):
                        at = GQ_HEADS * t + 2 * b
                        mm = pe.matmul(stat_bank[:, 0, at:at + 2], qk_sq[b][:, t * P:(t + 1) * P], c("head_ones"),
                                       start=True, stop=True)
                mm.then_inc(qk_sum, 1)

            def head_factors():
                pe.wait_ge(qk_root, 1)
                for h in range(GQ_HEADS):
                    b, rows = h // 2, slice(h % 2 * GQ_DIM, (h % 2 + 1) * GQ_DIM)
                    for t in range(NT):
                        at = GQ_HEADS * t + h
                        mm = pe.matmul(acc[(b + 1) // 2][rows, (b + 1) % 2, t * P:(t + 1) * P],
                                       root[:, 1, at:at + 1].to_broadcast([P, GQ_DIM]), c("ident"), start=True, stop=True)
                    if h in (1, 5, 9):
                        mm.then_inc(qk_spread, 1)

            def feature_sums(g):
                pe.wait_ge(drained, ROT["w_in"] + 4 + g // 2)
                if g:
                    pe.wait_ge(f_feat_copied, g)
                for n in range(NT):
                    mm = pe.matmul(rot[1][:, n, :], work[:, g, n * P:(n + 1) * P], dft_feature, start=True, stop=True)
                mm.then_inc(f_feat, 1)

            for j in range(5):
                square_tile(FIRST["w_in"] + j, rotating("w_in", j), xn_hi, xn_lo, ready=operand("mix") if j == 0 else None,
                            beside={**norm("mix"), 3: {5: head_sums}, 4: {4: head_factors}}.get(j, {}))
            pe.wait_ge(fourier_landed, FOURIER_DMAS)
            feature_sums(0)
            for n in range(NT):
                mm = pe.transpose(acc[3][:, 0, n * P:(n + 1) * P], gv_t[:, n * P:(n + 1) * P], c("ident"))
            mm.then_inc(v_turned, 1)
            part("gqa", 0, ks=(0, 2))
            pe.wait_ge(drained, ROT["w_in"] + 5)
            for g in range(4):
                f_s = probs[g % 2]
                pe.wait_ge(f_feat_copied, g + 1)
                if g:
                    pe.wait_ge(f_seq_copied, g)
                for n in range(NT):
                    pe.matmul(rot[2][:, 0, :], f_s[:, n, 0:P], dft_cos[:, n, :], start=n == 0, stop=False)
                    mm = pe.matmul(rot[2][:, 0, :], f_s[:, n, P:2 * P], dft_sin[:, n, :], start=False, stop=n == NT - 1)
                mm.then_inc(f_seq, 1)
                if g < 3:
                    feature_sums(g + 1)
                part("gqa", 0, ks=((2, 3), (3, 4), (4, 6), (6, 8))[g])
                pe.wait_ge(f_seq_copied, g + 1)
                if g:
                    pe.wait_ge(f_split, g)
                else:
                    pe.wait_ge(v_copied, 1)
                pe.matmul(acc[3][:, 1, :], f_w[:, g, :], probs_t[g % 2][:, 0, :], start=True, stop=True).then_inc(f_out, 1)
            attention("gqa")
            residual("w_out", lambda k: [(f_split, 4)] if k == 0 else [(a_split, UNIT0["gqa"] + 2 * (k - 3))] if k >= 4 else [])
            gate_up(1, "ffn2")
            down(1)

            for j in range(COUNT["conv_in"]):
                square_tile(FIRST["conv_in"] + j, rotating("conv_in", j), xn_hi, xn_lo, ready=operand("mix0") if j == 0 else None,
                            beside={1: {5: lambda: spread_factor("mix0")},
                                    2: {5: lambda: spread_diagonal(SUM["mix0"] + 2, 0)}}.get(j, {}))
                if j == 0:
                    sums("mix0")
            residual("conv_out", lambda k: [(y_split, k // 2 + 1)])

            def memory_attention(layer):
                kind = f"mem{layer}"
                first = PARTS[kind].index(("q", 0))
                for j in range(AHEAD[kind]):
                    part(kind, j, ready=operand(kind) if j == first else None, beside=norm(kind).get(j, {}))
                attention(kind)
                residual(f"mem_o{layer}", lambda k: [(a_split, UNIT0[kind] + k // 2 + 1)])

            memory_attention(0)
            gate_up(2, "ffn0")
            down(2)

            for j in range(AHEAD["moba"]):
                part("moba", j, ready={0: operand("kv"), 3: operand("mix1")}.get(j),
                     beside=norm("mix1").get(j, {}))
            attention("moba")
            residual("moba_o", lambda k: [(a_split, UNIT0["moba"] + k + 1)])
            memory_attention(1)
            gate_up(3, "ffn1")
            down(3, beside={(0, 5): lambda: sums("final", (0, 2)), (0, 7): lambda: sums("final", (2, 4))})
            sums("final", (4, KB))
            spread_factor("final")

        @block.scalar
        def _(act):
            act.dma_start(vec[:], vectors).then_inc(vec_landed, 16)
            act.wait_ge(ones_set, 2)
            act.activation(small[:, 0, 0, :], ones[:, 0:NT], ACT.Copy)

            def split(t, slot=None, turn=None):
                if slot is None:
                    if t >= TILES:
                        return
                    slot, turn = t % RING, t // RING
                act.wait_ge(landed[slot], 16 * turn)
                act.wait_ge(tile_done, t - (RING - 1))
                act.activation(w_hi[slot][:], raw[slot][:], ACT.Copy).then_inc(weight_hi, 1)

            def after(t):
                split(t + RING)

            def round_pair(b, src, gain, hi):
                for k in range(2 * b, 2 * b + 2):
                    e = act.activation(hi[:, k, :], src[:, k, :], ACT.Copy, scale=v(gain, k))
                e.then_inc(rounded, 1)

            def square_pair(b, src):
                act.activation(work[:, pair(b), :], src[:, pair(b), :], ACT.Square).then_inc(squared, 1)

            def squares(name, src):
                if SUM[name]:
                    act.wait_ge(summed, SUM[name])
                for b in range(KP):
                    square_pair(b, src)

            def stream(write, gain, name):
                for b in range(KP):
                    act.wait_ge(written, KP * WRITE[write] + b + 1)
                    round_pair(b, x, gain, xn_hi)
                    if write not in DOWNS and b < KP - 1:
                        after(FIRST[write] + b)
                squares(name, x)

            def gate_up(n):
                t0, r0 = FIRST[f"gu{n}"], ROT[f"gu{n}"]

                def hidden(j, buf, rows=P):
                    gate = gu_s[buf][0:rows, 0, :]
                    act.wait_ge(drained, j + (r0 + 1))
                    act.activation(gate, gate, ACT.Silu).then_inc(gated, 1)
                    act.wait_ge(whole, j + (FF * n + 1))
                    act.activation(h_hi[0:rows, j, :], gate, ACT.Copy).then_inc(h_rounded, 1)

                for j in range(PEEL):
                    for t in {0: [0, 1], 1: []}.get(j, [j]):
                        after(t0 + t)
                    hidden(j, j % 3)
                if n == 0:
                    act.wait_ge(mem_landed, 16)
                    squares("mem", mem)
                with act.Fori(0, turns(n)) as i:
                    for q in range(3):
                        t = t0 + PEEL + q
                        split(3 * i + (t + RING), t % RING, i + (t // RING + 1))
                        hidden(3 * i + (PEEL + q), (PEEL + q) % 3)
                for j in range(PEEL + 3 * turns(n), FF):
                    after(t0 + j)
                    hidden(j, j % 3, LAST if j == FF - 1 else P)

            def down_splits(n):
                t0 = FIRST[f"down{n}"]
                with act.Fori(0, FF // 2 // 3) as i:
                    for q in range(3):
                        t = t0 + 1 + q
                        split(3 * i + (t + RING), t % RING, i + (t // RING + 1))

            def attention(kind):
                u0, units, scale = UNIT0[kind], plan(kind), SCALE[kind]

                def exponentials(n):
                    u, a = u0 + n, units[n]
                    act.wait_ge(a_max, u + 1)
                    if u >= 2:
                        act.wait_ge(a_turned, u - 1)
                    for t in range(NT):
                        keys = (t + 1) * P if a["causal"] else S
                        e = act.activation(probs[u % 2][:, t, 0:keys], acc[u % 2][:, t, 0:keys], ACT.Exp, scale=scale,
                                           bias=small[:, u % 2, 1, t:t + 1], accum_out=small[:, u % 2, 2, t:t + 1])
                    e.then_inc(a_exp, 1)

                exponentials(0)
                exponentials(1)
                after(FIRST[kind] + AHEAD[kind] - 1)
                for n, a in enumerate(units):
                    u = u0 + n
                    if n == 0:
                        for j in ended(kind, n, 0):
                            after(FIRST[kind] + j)
                    act.wait_ge(a_turned, u + 1)
                    if u >= 2:
                        act.wait_ge(a_out, u - 1)
                    if a["causal"]:
                        act.activation(probs_t[u % 2][:, 0, :], acc[2][:, 0, :], ACT.Copy)
                        act.activation(probs_t[u % 2][:, 1, P:S], acc[2][:, 1, P:S], ACT.Copy).then_inc(a_turned_copied, 1)
                    else:
                        act.activation(probs_t[u % 2], acc[2][:], ACT.Copy).then_inc(a_turned_copied, 1)
                    if n + 2 < len(units):
                        exponentials(n + 2)
                    for j in (ended(kind, n, 0) if n else []) + ended(kind, n, 1):
                        after(FIRST[kind] + j)
                    act.wait_ge(a_out, u + 1)
                    b0, b1 = a["blocks"]
                    act.activation(h_hi[a["rows"], b0:b1, :], acc[3][a["rows"], 0:b1 - b0, :], ACT.Copy).then_inc(a_rounded, 1)

            def start(i, tile, k0, k1, last):
                act.wait_ge(start_landed[i], 16)
                act.activation(rows_of(w_hi[tile][:], k0, k1), rows_of(raw[tile][:], k0, k1),
                               ACT.Copy).then_inc(weight_hi if last else start_hi, 1)

            act.wait_ge(vec_landed, 16)
            for b in range(KP):
                start(b, 0, 2 * b, 2 * b + 2, b == KP - 1)
                act.wait_ge(x_landed[b], 16)
                round_pair(b, x, "ffn1_norm", xn_hi)
                if b == 1:
                    square_pair(0, x)
            square_pair(1, x)
            for i in range(2 * (RING - 1)):
                start(KP + i, 1 + i // 2, i % 2 * KB // 2, (i % 2 + 1) * KB // 2, i % 2 == 1)
                if i < 2:
                    square_pair(2 + i, x)
            gate_up(0)
            after(FIRST["down0"])
            for b in range(KP):
                round_pair(b, mem, "norm_memkv0", mn_hi)
            down_splits(0)
            stream("down0", "mix_norm", "mix")
            for t in range(-1, 2):
                after(FIRST["w_in"] + t)
            for g in range(3):
                act.wait_ge(drained, ROT["w_in"] + g + 1)
                src = gk_t if g == 0 else q_t[:, 2 * g - 2:2 * g, :]
                dst = (work[:, 4, :], work[:, 5:7, :], scratch[:, 6:8, :])[g]
                act.activation(dst, src, ACT.Square).then_inc(qk_squared, 1)
            after(FIRST["w_in"] + 2)

            def features_copied(g):
                act.wait_ge(f_feat, g + 1)
                if g >= 2:
                    act.wait_ge(f_seq, g - 1)
                act.activation(probs[g % 2], rot[1][:], ACT.Copy).then_inc(f_feat_copied, 1)

            features_copied(0)
            act.wait_ge(v_turned, 1)
            act.activation(v_s[:, :, 0:P], acc[3][:, 0, :].rearrange("p (t d) -> p t d", t=NT), ACT.Copy).then_inc(v_copied, 1)
            after(FIRST["w_in"] + 3)
            for g in range(4):
                act.wait_ge(f_seq, g + 1)
                if g >= 2:
                    act.wait_ge(f_out, g - 1)
                act.activation(probs_t[g % 2][:, 0, :], rot[2][:, 0, :], ACT.Copy).then_inc(f_seq_copied, 1)
                if g < 3:
                    features_copied(g + 1)
                act.wait_ge(f_out, g + 1)
                act.activation(h_hi[:, g, :], acc[3][:, 1, :], ACT.Identity, bias=v("fnet_b", g)).then_inc(f_rounded, 1)
                if g == 1:
                    after(FIRST["w_in"] + 4)
            attention("gqa")
            stream("w_out", "ffn2_norm", "ffn2")
            after(FIRST["gu1"] - 1)
            gate_up(1)
            after(FIRST["down1"])
            act.wait_ge(trig_ready, 1)
            act.activation(m_sin[:], scratch[0:32, 6, :], ACT.Sin).then_inc(trig_done, 1)
            act.activation(m_cos[:], scratch[0:32, 7, :], ACT.Sin).then_inc(trig_done, 1)
            down_splits(1)
            stream("down1", "gain2", "mix0")
            after(FIRST["conv_in"] - 1)
            for p in range(KP):
                for j in range(3):
                    after(FIRST["conv_in"] + 3 * p + j)
                act.wait_ge(y_whole, p + 1)
                act.activation(h_hi[:, pair(p), :], tap_s, ACT.Copy).then_inc(y_rounded, 1)
            stream("conv_out", "norm_mem0", "mem0")
            after(FIRST["mem0"] - 1)
            for j in range(AHEAD["mem0"] - 1):
                after(FIRST["mem0"] + j)
            attention("mem0")
            stream("mem_o0", "norm_ffn0", "ffn0")
            after(FIRST["gu2"] - 1)
            gate_up(2)
            after(FIRST["down2"])
            for b in range(KP):
                round_pair(b, mem, "norm_memkv1", mn_hi)
            down_splits(2)
            stream("down2", "kv_norm", "mix1")
            after(FIRST["moba"] - 1)
            after(FIRST["moba"])
            for b in range(KP):
                round_pair(b, x, "norm_mix1", h_hi[:, KB:2 * KB, :])
            for j in range(1, AHEAD["moba"] - 1):
                after(FIRST["moba"] + j)
            attention("moba")
            stream("moba_o", "norm_mem1", "mem1")
            after(FIRST["mem1"] - 1)
            for j in range(AHEAD["mem1"] - 1):
                after(FIRST["mem1"] + j)
            attention("mem1")
            stream("mem_o1", "norm_ffn1", "ffn1")
            after(FIRST["gu3"] - 1)
            gate_up(3)
            for t in range(FIRST["down3"], TILES - RING):
                after(t)
            act.wait_ge(summed, SUM["final"])
            for b in range(KP):
                act.wait_ge(written, KP * WRITE["down3"] + b + 1)
                square_pair(b, x)
            for k in range(KB):
                e = act.activation(q_t[:, k, :], x[:, k, :], ACT.Copy, scale=v("norm_final", k))
            e.then_inc(out_gained, 1)

        @block.vector
        def _(dve):
            links = [0]

            def link(e):
                links[0] += 1
                e.then_inc(linked, 1)
                dve.wait_ge(linked, links[0])

            def split(t, slot=None):
                if slot is None:
                    if t >= TILES:
                        return
                    slot = t % RING
                dve.wait_ge(weight_hi, t + 1)
                dve.tensor_tensor(w_lo[slot][:], raw[slot][:], w_hi[slot][:].bitcast(F32), ALU.subtract).then_inc(weight_lo, 1)

            def after(t):
                split(t + RING - 1)

            def rest_pair(name, b, src, gain, hi, lo):
                dve.wait_ge(rounded, KP * OPERAND[name] + b + 1)
                for k in range(2 * b, 2 * b + 2):
                    e = dve.scalar_tensor_tensor(lo[:, k, :], src[:, k, :], v(gain, k), hi[:, k, :].bitcast(F32),
                                                 ALU.mult, ALU.subtract)
                e.then_inc(split_done, 1)

            def stream(write, gain, name, scale=1.0):
                for b in range(KP + 1):
                    if b < KP:
                        if write in DOWNS and b < KP - 1:
                            dve.wait_ge(acc_done, (KP - 1) * DOWNS[write] + b + 1)
                        else:
                            dve.wait_ge(tile_done, FIRST[write] + (COUNT[write] if write in DOWNS else b + 1))
                        dve.scalar_tensor_tensor(x[:, pair(b), :], acc[b][:], scale, x[:, pair(b), :],
                                                 ALU.mult, ALU.add).then_inc(written, 1)
                    if b and gain:
                        rest_pair(name, b - 1, x, gain, xn_hi, xn_lo)
                    if write not in DOWNS and b < KP - 1:
                        after(FIRST[write] + b)

            def inverse_root(n, done=None):
                m, y, t = (root[:, i, 0:n] for i in range(3))
                link(dve.tensor_scalar(y.bitcast(I32), m.bitcast(I32), 1, None, ALU.logical_shift_right))
                link(dve.tensor_scalar(y.bitcast(I32), y.bitcast(I32), -1.0, ROOT_GUESS, ALU.mult, ALU.add))
                for step in range(ROOT_STEPS):
                    link(dve.tensor_tensor(t, y, y, ALU.mult))
                    link(dve.scalar_tensor_tensor(t, t, -0.5, m, ALU.mult, ALU.mult))
                    e = dve.scalar_tensor_tensor(y, t, 1.5, y, ALU.add, ALU.mult)
                    if done is not None and step == ROOT_STEPS - 1:
                        e.then_inc(done, 1)
                    else:
                        link(e)

            def on_diagonal(col):
                for t in range(NT):
                    e = dve.tensor_scalar(diag[:, t, :], c("ident"), col[:, t:t + 1], None, ALU.mult)
                e.then_inc(factor, 1)

            def factors(name, col):
                dve.wait_ge(summed, SUM[name] + 1)
                link(dve.tensor_scalar(root[:, 0, 0:NT], stat_bank[:, 0, 0:NT], 1.0 / D, EPS, ALU.mult, ALU.add))
                inverse_root(NT)
                link(dve.tensor_copy(col[:], root[:, 1, 0:NT]))
                on_diagonal(col)

            def spread_to(name, r):
                dve.wait_ge(spread, SUM[name] + (2 if SUM[name] > SUM["mix0"] else 1))
                dve.tensor_copy(r[:], stat_bank[:, 1, :]).then_inc(spread_read, 1)
                dve.wait_ge(spread_read, SUM[name] + 1)

            def gate_up(n, name):
                t0, r0 = FIRST[f"gu{n}"], ROT[f"gu{n}"]

                def scaled(t, buf, block_of):
                    dve.wait_ge(tile_done, t + 1)
                    dve.tensor_tensor(gu_s[buf], rot[block_of][:], both(r_x[:]), ALU.mult).then_inc(drained, 1)

                def scaled_halves(t, buf, block_of):
                    dve.wait_ge(tile_done, t + 1)
                    for i in range(2):
                        r = slice(i * LAST, (i + 1) * LAST)
                        e = dve.tensor_tensor(gu_s[buf][0:LAST, i, :], rot[block_of][r, 0, :], r_x[r, :], ALU.mult)
                    e.then_inc(drained, 1)

                def multiplied(j, buf, rows=P):
                    gate, up = (gu_s[buf][0:rows, i, :] for i in range(2))
                    dve.wait_ge(gated, j + (FF * n + 1))
                    dve.tensor_tensor(gate, gate, up, ALU.mult).then_inc(whole, 1)

                def rest(j, buf, count, rows=P):
                    dve.wait_ge(h_rounded, count)
                    dve.tensor_tensor(h_lo[0:rows, j, :], gu_s[buf][0:rows, 0, :], h_hi[0:rows, j, :].bitcast(F32),
                                      ALU.subtract).then_inc(h_split, 1)

                if n:
                    after(t0)
                factors(name, col_x)
                after(t0 + 1)
                spread_to(name, r_x)
                for j in range(PEEL):
                    scaled(t0 + j, j % 3, (r0 + j) % 3)
                    if j in (0, 3):
                        after(t0 + max(j, 2))
                    multiplied(j, j % 3)
                    if j:
                        rest(j - 1, (j - 1) % 3, FF * n + j)
                with dve.Fori(0, turns(n)) as i:
                    for q in range(3):
                        j, t = PEEL + q, t0 + PEEL + q
                        scaled(3 * i + t, j % 3, (r0 + j) % 3)
                        split(3 * i + (t + RING - 1), (t + RING - 1) % RING)
                        multiplied(3 * i + j, j % 3)
                        rest(3 * i + (j - 1), (j - 1) % 3, 3 * i + (FF * n + j))
                for j in range(PEEL + 3 * turns(n), FF):
                    last = j == FF - 1
                    (scaled_halves if last else scaled)(t0 + j, j % 3, (r0 + j) % 3)
                    after(t0 + j)
                    multiplied(j, j % 3, LAST if last else P)
                    rest(j - 1, (j - 1) % 3, FF * n + j)
                rest(FF - 1, (FF - 1) % 3, FF * (n + 1), LAST if n < 2 else P)

            def down_splits(n):
                t0 = FIRST[f"down{n}"]
                with dve.Fori(0, FF // 2 // 3) as i:
                    for q in range(3):
                        t = t0 + 1 + q + RING - 1
                        split(3 * i + t, t % RING)

            def part(kind, j):
                what, i = PARTS[kind][j]
                t, src = FIRST[kind] + j, rot[(ROT[kind] + j) % 3]
                of_memory = what == "m" if kind == "moba" else what != "q"
                dve.wait_ge(tile_done, t + 1)
                if what == "v":
                    col = col_m if of_memory else col_x
                    for n in range(NT):
                        e = dve.tensor_scalar(v_s[:, n, 2 * P * i:2 * P * (i + 1)], src[:, n, :], col[:, n:n + 1], None, ALU.mult)
                else:
                    dst = q_t if what == "q" else k_t
                    e = dve.tensor_tensor(dst[:, pair(i), :], src[:], both((r_m if of_memory else r_x)[:]), ALU.mult)
                e.then_inc(drained, 1)

            def swap_halves(what, j):
                g, part_t = ROPES.index((what, j)), k_t if what == "k" else q_t
                if g >= 2:
                    dve.wait_ge(rope_done, g - 1)
                dve.wait_ge(drained, ROT["moba"] + MOBA.index((what, j)) + 1)
                dve.stream_shuffle(rope_partner(g), part_t[0:32, pair(j), :], HALVES_SWAPPED).then_inc(rope_swapped, 1)

            def attention(kind):
                u0, units, scale = UNIT0[kind], plan(kind), SCALE[kind]

                def maxima(n):
                    u, a = u0 + n, units[n]
                    top, low = small[:, u % 2, 0, :], small[:, u % 2, 1, :]
                    dve.wait_ge(a_scores, u + 1)
                    if a["causal"]:
                        own = [acc[u % 2][:, t, t * P:(t + 1) * P] for t in range(NT)]
                        dve.tensor_tensor(own[0], own[0], c("causal"), ALU.add)
                        link(dve.tensor_tensor(own[1], own[1], c("causal"), ALU.add))
                        for t in range(NT):
                            e = dve.tensor_reduce(top[:, t:t + 1], acc[u % 2][:, t, 0:(t + 1) * P], AX.X, ALU.max)
                        link(e)
                    else:
                        link(dve.tensor_reduce(top, acc[u % 2][:], AX.X, ALU.max))
                    dve.tensor_scalar(low, top, -scale, None, ALU.mult).then_inc(a_max, 1)

                def normalise(n):
                    u, a = u0 + n, units[n]
                    dve.wait_ge(a_exp, u + 1)
                    link(dve.reciprocal(small[:, u % 2, 3, :], small[:, u % 2, 2, :]))
                    for t in range(NT):
                        keys = (t + 1) * P if a["causal"] else S
                        pr = probs[u % 2][:, t, 0:keys]
                        e = dve.tensor_scalar(pr, pr, small[:, u % 2, 3, t:t + 1], None, ALU.mult)
                    e.then_inc(a_probs, 1)

                def rest(n):
                    u, a = u0 + n, units[n]
                    b0, b1 = a["blocks"]
                    dve.wait_ge(a_rounded, u + 1)
                    dve.tensor_tensor(h_lo[a["rows"], b0:b1, :], acc[3][a["rows"], 0:b1 - b0, :],
                                      h_hi[a["rows"], b0:b1, :].bitcast(F32), ALU.subtract).then_inc(a_split, 1)

                def pieces(n, i):
                    for j in ended(kind, n, i):
                        part(kind, j)
                        if kind == "moba" and MOBA[j] in ROPES:
                            swap_halves(*MOBA[j])
                        after(FIRST[kind] + j)

                maxima(0)
                maxima(1)
                normalise(0)
                after(FIRST[kind] + AHEAD[kind] - 1)
                for n in range(len(units)):
                    if n:
                        rest(n - 1)
                    pieces(n, 0)
                    if n + 1 < len(units):
                        normalise(n + 1)
                    if n + 2 < len(units):
                        maxima(n + 2)
                    pieces(n, 1)
                rest(len(units) - 1)

            def start(tile, k0, k1, sem_hi, count, sem_lo):
                dve.wait_ge(sem_hi, count)
                dve.tensor_tensor(rows_of(w_lo[tile][:], k0, k1), rows_of(raw[tile][:], k0, k1),
                                  rows_of(w_hi[tile][:], k0, k1).bitcast(F32), ALU.subtract).then_inc(sem_lo, 1)

            dve.wait_ge(vec_landed, 16)
            for b in range(KP):
                start(0, 2 * b, 2 * b + 2, *((start_hi, b + 1, start_lo) if b < KP - 1 else (weight_hi, 1, weight_lo)))
                rest_pair("x0", b, x, "ffn1_norm", xn_hi, xn_lo)
            for t in range(1, RING):
                start(t, 0, KB // 2, start_hi, KP - 1 + t, start_lo)
                start(t, KB // 2, KB, weight_hi, t + 1, weight_lo)
            a, b = VCOL["final_norm"][0], VCOL["norm_mix0"][0]
            dve.tensor_tensor(gain2[:], vec[:, a:a + KB], vec[:, b:b + KB], ALU.mult)
            dve.tensor_tensor(weigh[:, :, 1], vec[:, a:a + KB], vec[:, a:a + KB], ALU.mult)
            dve.wait_ge(const_landed, CONST_DMAS)
            gate_up(0, "x0")
            after(FIRST["down0"])
            dve.wait_ge(mem_landed, 16)
            factors("mem", col_m)
            for b in range(KP):
                rest_pair("memkv0", b, mem, "norm_memkv0", mn_hi, mn_lo)
            down_splits(0)
            spread_to("mem", r_m)
            stream("down0", "mix_norm", "mix", 0.5)
            after(FIRST["w_in"] - 1)

            def qkf(j):
                src = rot[(ROT["w_in"] + j) % 3]
                dve.wait_ge(tile_done, FIRST["w_in"] + j + 1)
                if j == 0:
                    dve.tensor_tensor(gk_t, src[:, 0, :], r_x[:], ALU.mult)
                    e = dve.tensor_tensor(gv_t, src[:, 1, :], r_x[:], ALU.mult)
                else:
                    dst = q_t[:, 2 * j - 2:2 * j, :] if j < 3 else work[:, 2 * j - 6:2 * j - 4, :]
                    e = dve.tensor_tensor(dst, src[:], both(r_x[:]), ALU.mult)
                e.then_inc(drained, 1)

            after(FIRST["w_in"])
            factors("mix", col_x)
            after(FIRST["w_in"] + 1)
            spread_to("mix", r_x)
            def head_group(g):
                return q_t[:, 5:6, :] if g == 0 else q_t[:, 2 * g - 2:2 * g, :]

            def head_norm(g):
                inv = acc[0][:, 1:2, :] if g == 0 else acc[g][:]
                dve.wait_ge(qk_spread, g + 1)
                dve.scalar_tensor_tensor(head_group(g), head_group(g), v("q_norm" if g else "k_norm"), inv,
                                         ALU.mult, ALU.mult).then_inc(qk_normed, 1)

            def head_rope(g):
                part_t, n = head_group(g), 1 if g == 0 else 2
                partner = work[:, 4:4 + n, :]
                dve.wait_ge(qk_normed, g + 1)
                if g:
                    dve.wait_ge(qk_done, g)
                link(dve.stream_shuffle(partner, part_t, HALVES_SWAPPED))
                dve.tensor_tensor(part_t, part_t, both(c("axial_cos"), n), ALU.mult)
                link(dve.tensor_tensor(partner, partner, both(c("axial_sin"), n), ALU.mult))
                dve.tensor_tensor(part_t, part_t, partner, ALU.add).then_inc(qk_done, 1)

            def group_rest(g):
                dve.wait_ge(f_rounded, g + 1)
                dve.scalar_tensor_tensor(h_lo[:, g, :], acc[3][:, 1, :], v("fnet_b", g), h_hi[:, g, :].bitcast(F32),
                                         ALU.add, ALU.subtract).then_inc(f_split, 1)

            for j in range(3):
                qkf(j)
            after(FIRST["w_in"] + 2)
            dve.wait_ge(qk_sum, 1)
            link(dve.tensor_scalar(root[:, 0, :], stat_bank[:, 0, 0:2 * GQ_HEADS], 1.0 / GQ_DIM, EPS, ALU.mult, ALU.add))
            inverse_root(2 * GQ_HEADS, done=qk_root)
            qkf(3)
            after(FIRST["w_in"] + 3)
            for g in range(3):
                head_norm(g)
            qkf(4)
            head_rope(0)
            head_rope(1)
            group_rest(0)
            head_rope(2)
            group_rest(1)
            after(FIRST["w_in"] + 4)
            group_rest(2)
            group_rest(3)
            part("gqa", 0)
            attention("gqa")
            stream("w_out", "ffn2_norm", "ffn2")
            after(FIRST["gu1"] - 1)
            gate_up(1, "ffn2")
            after(FIRST["down1"])
            turn, red, quarter = scratch[0:32, 5, :], scratch[0:32, 6, :], scratch[0:32, 7, :]
            freq = con[0:32, CCOL["inv_freq"][0]:CCOL["inv_freq"][1]]
            link(dve.tensor_copy(turn, pos))
            link(dve.tensor_scalar(red, turn, freq, None, ALU.mult))
            link(dve.tensor_scalar(turn, red, 1.0 / TWO_PI, ROUND, ALU.mult, ALU.add))
            link(dve.tensor_scalar(turn, turn, ROUND, None, ALU.subtract))
            for piece in TURN:
                link(dve.scalar_tensor_tensor(red, turn, -piece, red, ALU.mult, ALU.add))
            link(dve.scalar_tensor_tensor(quarter, red, -1.0, red, ALU.mult, ALU.max))
            link(dve.tensor_scalar(red, red, -PI_BELOW, PI_BELOW, ALU.max, ALU.min))
            dve.tensor_scalar(quarter, quarter, -1.0, float(np.pi / 2), ALU.mult, ALU.add).then_inc(trig_ready, 1)
            down_splits(1)
            stream("down1", "gain2", "mix0", 0.5)
            after(FIRST["conv_in"] - 1)

            dve.wait_ge(summed, SUM["mix0"] + 1)
            sq = stat_bank[:, 0, 0:2 * NT].rearrange("p (t w) -> p t w", w=2)
            link(dve.tensor_scalar(root[:, 0, 0:NT], sq[:, :, 0], 1.0 / D, EPS, ALU.mult, ALU.add))
            link(dve.tensor_scalar(root[:, 2, 0:NT], root[:, 0, 0:NT], EPS, None, ALU.mult))
            link(dve.scalar_tensor_tensor(root[:, 0, NT:2 * NT], sq[:, :, 1], 1.0 / D, root[:, 2, 0:NT], ALU.mult, ALU.add))
            inverse_root(2 * NT)
            dve.tensor_copy(col_1[:], root[:, 1, 0:NT])
            link(dve.tensor_copy(col_x[:], root[:, 1, NT:2 * NT]))
            on_diagonal(col_x)
            after(FIRST["conv_in"])
            dve.wait_ge(spread, SUM["mix0"] + 1)
            link(dve.tensor_copy(r_x[:], stat_bank[:, 1, :]))
            on_diagonal(col_1)
            dve.wait_ge(pads_set, 1)
            for p in range(KP):
                for m in range(2):
                    k, j = 2 * p + m, 3 * p + m
                    dve.wait_ge(tile_done, FIRST["conv_in"] + j + 1)
                    dve.tensor_tensor(conv_s[0], rot[(ROT["conv_in"] + j) % 3][:], both(r_x[:]), ALU.mult).then_inc(drained, 1)
                    if j:
                        after(FIRST["conv_in"] + j)
                    dve.wait_ge(drained, ROT["conv_in"] + j + 1)
                    z, tap = z_s[:, m, :], tap_s[:, m, :]
                    if m == 0 and p:
                        dve.wait_ge(y_split, p)
                    link(dve.tensor_tensor(z[:, 2:S + 2], conv_s[0][:, 0, :], conv_s[0][:, 1, :], ALU.mult))
                    link(dve.tensor_scalar(tap, z[:, 2:S + 2], v("conv_w", 2 * KB + k), None, ALU.mult))
                    for w in (1, 0):
                        link(dve.scalar_tensor_tensor(tap, z[:, w:S + w], v("conv_w", w * KB + k), tap, ALU.mult, ALU.add))
                j = 3 * p + 2
                dve.wait_ge(tile_done, FIRST["conv_in"] + j + 1)
                dve.tensor_tensor(conv_s[1], rot[(ROT["conv_in"] + j) % 3][:], both(r_x[:]), ALU.mult).then_inc(drained, 1)
                after(FIRST["conv_in"] + j)
                dve.wait_ge(drained, ROT["conv_in"] + j + 1)
                dve.tensor_tensor(tap_s, tap_s, conv_s[1], ALU.mult).then_inc(y_whole, 1)
                dve.wait_ge(y_rounded, p + 1)
                dve.tensor_tensor(h_lo[:, pair(p), :], tap_s, h_hi[:, pair(p), :].bitcast(F32), ALU.subtract).then_inc(y_split, 1)
                if p == 0:
                    dve.wait_ge(spread, SUM["mix0"] + 2)
                for k in range(2 * p, 2 * p + 2):
                    e = dve.scalar_tensor_tensor(x[:, k, :], x[:, k, :], v("final_norm", k), stat_bank[:, 0, :], ALU.mult, ALU.mult)
            e.then_inc(spread_read, 1)
            stream("conv_out", "norm_mem0", "mem0")
            after(FIRST["mem0"] - 1)

            def memory_attention(kind):
                ahead = PARTS[kind][0][0] != "q"
                if ahead:
                    part(kind, 0)
                after(FIRST[kind])
                factors(kind, col_x)
                after(FIRST[kind] + 1)
                spread_to(kind, r_x)
                for j in range(int(ahead), AHEAD[kind]):
                    part(kind, j)
                    if 1 < j < AHEAD[kind] - 1:
                        after(FIRST[kind] + j)
                attention(kind)

            memory_attention("mem0")
            stream("mem_o0", "norm_ffn0", "ffn0")
            after(FIRST["gu2"] - 1)
            gate_up(2, "ffn0")
            after(FIRST["down2"])
            for b in range(KP):
                rest_pair("memkv1", b, mem, "norm_memkv1", mn_hi, mn_lo)
            down_splits(2)
            stream("down2", "kv_norm", "kv")
            after(FIRST["moba"] - 1)

            after(FIRST["moba"])
            factors("mix1", col_x)
            after(FIRST["moba"] + 1)

            def query_operand(b):
                rest_pair("mix1", b, x, "norm_mix1", h_hi[:, KB:2 * KB, :], h_lo[:, KB:2 * KB, :])

            query_operand(0)
            spread_to("mix1", r_x)
            part("moba", 0)
            for b in range(1, KP):
                query_operand(b)
            part("moba", 1)
            swap_halves("k", 0)
            after(FIRST["moba"] + 2)
            part("moba", 2)
            part("moba", 3)
            swap_halves("q", 0)
            swap_halves("k", 1)
            after(FIRST["moba"] + 3)
            part("moba", 4)
            swap_halves("q", 1)
            attention("moba")
            stream("moba_o", "norm_mem1", "mem1")
            after(FIRST["mem1"] - 1)
            memory_attention("mem1")
            stream("mem_o1", "norm_ffn1", "ffn1")
            after(FIRST["gu3"] - 1)
            gate_up(3, "ffn1")
            for t in range(FIRST["down3"], TILES - RING + 1):
                after(t)
            stream("down3", None, "final")
            factors("final", col_x)
            dve.wait_ge(spread, SUM["final"] + 2)
            dve.wait_ge(out_gained, 1)
            for b in range(KP):
                dve.tensor_tensor(work[:, pair(b), :], q_t[:, pair(b), :], both(stat_bank[:, 1, :]), ALU.mult).then_inc(out_ready, 1)


def column_blocks(w):
    n = w.shape[1] // (2 * P)
    return w.reshape(KB, P, n, 2, P).transpose(2, 1, 3, 0, 4).reshape(n, P, TILE, P)


def row_blocks(w):
    n = w.shape[0] // (2 * P)
    return w.reshape(n, 2, P, KB, P).transpose(0, 2, 1, 3, 4).reshape(n, P, TILE, P)


def gate_up_blocks(gate, up):
    whole = gate.shape[1] // P * P
    both = np.stack([a[:, :whole].reshape(D, -1, P) for a in (gate, up)], axis=2).reshape(D, 2 * whole)
    both = np.concatenate([both, gate[:, whole:], up[:, whole:]], axis=1)
    return column_blocks(np.pad(both, ((0, 0), (0, 2 * FF * P - both.shape[1]))))


def down_blocks(w):
    return row_blocks(np.pad(w, ((0, FF * P - w.shape[0]), (0, 0))))


def feature_major(a):
    return np.ascontiguousarray(a.T.reshape(KB, P, a.shape[0]).transpose(1, 0, 2))


def constants():
    def dft(n):
        a = 2 * np.pi * (np.outer(np.arange(n), np.arange(n)) % n) / n
        return np.cos(a), np.sin(a)

    cf, sf = dft(P)
    cs, ss = dft(S)
    ortho = 1.0 / np.sqrt(S * P)
    by_tile = lambda a: a.reshape(NT, P, S).transpose(1, 0, 2).reshape(P, NT * S)
    i = np.arange(P)
    sign = np.where(i % 32 < 16, -1.0, 1.0)[:, None]
    grid_w, axis_dim = 64, GQ_DIM // 2
    inv = (10000.0 ** (-np.arange(0, axis_dim, 2) / axis_dim)).astype(np.float32)
    tok = np.arange(S)
    place = np.where((i % GQ_DIM < axis_dim)[:, None], (tok // grid_w)[None], (tok % grid_w)[None]).astype(np.float32)
    ang = (place * inv[i % 16][:, None]).astype(np.float32).astype(np.float64)
    freq = np.zeros((P, 1))
    freq[:32, 0] = sign[:32, 0] * 500000.0 ** (-2.0 * (np.arange(32) % 16) / 32)
    table = dict(
        dft_feature=np.concatenate([cf, sf], 1), dft_cos=by_tile(cs * ortho), dft_sin=by_tile(-ss * ortho),
        head_ones=(i[:, None] // GQ_DIM == np.arange(2)[None]), ident=np.eye(P), axial_cos=np.cos(ang), axial_sin=sign * np.sin(ang),
        causal=np.where(i[:, None] >= i[None], 0.0, -1e30), inv_freq=freq)
    return [np.concatenate([np.asarray(table[n], np.float32) for n, _ in names], axis=1) for names in (CONSTS, FOURIER)]


def kernel(**inputs):
    import concourse.bacc as bacc
    from concourse.bass_utils import run_bass_kernel_spmd

    a = {n: np.asarray(t) for n, t in inputs.items()}
    heads = [h for b in range(4) for h in (b, b + 4)]
    head_cols = np.concatenate([np.arange(h * GQ_DIM, (h + 1) * GQ_DIM) for h in heads])
    f, q, k, val = np.split(a["w_in"], [512, 1024, 1152], axis=1)
    w_in = np.concatenate([k, val, q[:, head_cols], f], axis=1)
    w_out = np.concatenate([a["w_out"][:512], a["w_out"][512:][head_cols]], axis=0)
    gate_b, gate_c, u = (t.reshape(D, KP, 2, 1, P) for t in np.split(a["conv_w_in_2"][0], 3, axis=1))
    conv_in = np.concatenate([np.concatenate([gate_c, u], 3).reshape(D, KP, 4, P), gate_b.reshape(D, KP, 2, P)], 2).reshape(D, 3 * D)
    gu2 = [np.split(w, 2, axis=1) for w in a["ffn_w_gu_2"]]
    mem_kv = [column_blocks(w) for w in a["mem_w_kv_2"]]
    tiles = {
        "gu0": gate_up_blocks(a["ffn1_w_gate"], a["ffn1_w_up"]), "down0": down_blocks(a["ffn1_w_down"]),
        "gu1": gate_up_blocks(a["ffn2_w_gate"], a["ffn2_w_up"]), "down1": down_blocks(a["ffn2_w_down"]),
        "gu2": gate_up_blocks(*gu2[0]), "down2": down_blocks(a["ffn_w_down_2"][0]),
        "gu3": gate_up_blocks(*gu2[1]), "down3": down_blocks(a["ffn_w_down_2"][1]),
        "w_in": column_blocks(w_in), "w_out": column_blocks(w_out),
        "conv_in": column_blocks(conv_in), "conv_out": column_blocks(a["conv_w_out_2"][0]),
        "mem_o0": column_blocks(a["mem_w_o_2"][0]), "mem_o1": column_blocks(a["mem_w_o_2"][1]),
        "moba_o": column_blocks(a["moba_w_o_2"][0]),
    }
    key, value = slice(0, KP), slice(KP, 2 * KP)
    moba_kv = column_blocks(a["w_kv_2"])
    sources = {
        "gqa": {"k": mem_kv[0][key]},
        "mem0": {"q": column_blocks(a["mem_w_q_2"][0]), "v": mem_kv[0][value]},
        "moba": {"k": moba_kv[key], "q": column_blocks(a["moba_w_q_2"][0]), "v": moba_kv[value], "m": mem_kv[1][key]},
        "mem1": {"k": mem_kv[1][key], "q": column_blocks(a["mem_w_q_2"][1]), "v": mem_kv[1][value]},
    }
    for kind, parts in PARTS.items():
        tiles[kind] = np.stack([sources[kind][what][i] for what, i in parts])
    weights = np.concatenate([tiles[n] for n, _ in STREAM], axis=0)
    by_block = lambda t: t.reshape(-1, P).T
    vec = {
        "ffn1_norm": a["ffn1_norm"], "mix_norm": a["mix_norm"], "ffn2_norm": a["ffn2_norm"], "final_norm": a["final_norm"],
        "norm_mix0": a["norm_mix_2"][0], "norm_mix1": a["norm_mix_2"][1], "norm_mem0": a["norm_mem_2"][0],
        "norm_mem1": a["norm_mem_2"][1], "norm_memkv0": a["norm_memkv_2"][0], "norm_memkv1": a["norm_memkv_2"][1],
        "norm_ffn0": a["norm_ffn_2"][0], "norm_ffn1": a["norm_ffn_2"][1], "norm_final": a["norm_final_2"],
        "kv_norm": a["kv_norm_2"], "conv_w": a["conv_w_2"][0], "fnet_b": a["fnet_b"],
        "q_norm": np.concatenate([a["q_norm"]] * 2), "k_norm": np.concatenate([a["k_norm"]] * 2),
    }
    consts, fourier = constants()
    arrays = {
        "weights": weights, "x_t": feature_major(a["x"][0]), "mem_t": feature_major(a["mem_2"][0]),
        "vectors": np.ascontiguousarray(np.concatenate([by_block(vec[n]) for n, _ in VECTORS], axis=1)),
        "consts": consts, "fourier": fourier,
        "fnet_w": np.ascontiguousarray(a["fnet_w"].transpose(1, 0, 2)),
        "positions": np.ascontiguousarray(np.broadcast_to(a["positions_2"].astype(np.int32), (32, S))),
    }
    nc = bacc.Bacc("TRN2", target_bir_lowering=False, num_devices=1, dynamic_dma_scratch_size=1024)
    args = [nc.dram_tensor(n, t.shape, mybir.dt.from_np(t.dtype), kind="ExternalInput").ap() for n, t in arrays.items()]
    args.append(nc.dram_tensor("out_t", (P, KB, S), F32, kind="ExternalOutput").ap())
    program(nc, *args)
    r = run_bass_kernel_spmd(nc, [arrays], core_ids=[0])
    out = r.results[0]["out_t"]
    return np.ascontiguousarray(out.transpose(1, 0, 2).reshape(D, S).T)[None]
```
